# Optimizing a Trainium2 kernel written in Bass

```python
import jax, jax.numpy as jnp
from jax import lax
import numpy as np

D_MODEL = 2048
BATCH = 1
SEQ = 256
DEPTH = 1

CHUNK = 64
EPS = 1e-6
POOL_WIDTH = 1024
POOL_WINDOWS = (2, 4, 8, 16)
N_POOL_GROUPS = 4
POOL_GROUP = POOL_WIDTH // N_POOL_GROUPS
N_Q_HEADS = 16
N_KV_HEADS = 4
HEAD_DIM = 64
ATTN_WIDTH = N_Q_HEADS * HEAD_DIM
KV_WIDTH = N_KV_HEADS * HEAD_DIM
WINDOW = 128
WINDOW_CHUNKS = WINDOW // CHUNK
CONV_WIDTH = 1024
CONV_KERNEL = 31
N_BRANCHES = 3
IN_SPLITS = (POOL_WIDTH, POOL_WIDTH, ATTN_WIDTH, KV_WIDTH, KV_WIDTH, ATTN_WIDTH,
             CONV_WIDTH, CONV_WIDTH, CONV_WIDTH, N_BRANCHES * D_MODEL)
IN_WIDTH = 2 * POOL_WIDTH + 2 * ATTN_WIDTH + 2 * KV_WIDTH + 3 * CONV_WIDTH + N_BRANCHES * D_MODEL

kernel_name = "hybrid_pool_swa_conformer_parallel"

def rms_norm(x, g):
    xf = x.astype(jnp.float32)
    y = xf * lax.rsqrt(jnp.mean(xf * xf, axis=-1, keepdims=True) + EPS)
    return y.astype(x.dtype) * g

def layer_norm(x, g, b):
    xf = x.astype(jnp.float32)
    mu = jnp.mean(xf, axis=-1, keepdims=True)
    var = jnp.mean(jnp.square(xf - mu), axis=-1, keepdims=True)
    return ((xf - mu) * lax.rsqrt(var + EPS)).astype(x.dtype) * g + b

def multiscale_pool(u, pool_w, pool_scale):
    B, S, _ = u.shape
    ug = u.astype(jnp.float32).reshape(B, S, N_POOL_GROUPS, POOL_GROUP)
    cs = jnp.cumsum(ug, axis=1)
    t = jnp.arange(S)
    means = []
    for gi, w in enumerate(POOL_WINDOWS):
        c_g = cs[:, :, gi]
        prev = jnp.pad(c_g, ((0, 0), (w, 0), (0, 0)))[:, :S]
        cnt = jnp.minimum(t + 1, w).astype(jnp.float32)[None, :, None]
        means.append((c_g - prev) / cnt)
    mixed = (jnp.stack(means, axis=2) - ug).astype(u.dtype)
    y = jnp.einsum('bsgc,gcd->bsgd', mixed, pool_w)
    return y.reshape(B, S, POOL_WIDTH) * pool_scale

def window_attention(q, k, v, sink):
    B, S = q.shape[:2]
    nc = S // CHUNK
    grp = N_Q_HEADS // N_KV_HEADS
    qc = q.reshape(B, nc, CHUNK, N_KV_HEADS, grp, HEAD_DIM)
    pad = WINDOW_CHUNKS * CHUNK

    def band(t):
        tp = jnp.pad(t, ((0, 0), (pad, 0), (0, 0), (0, 0)))
        tp = tp.reshape(B, nc + WINDOW_CHUNKS, CHUNK, N_KV_HEADS, HEAD_DIM)
        return jnp.concatenate([tp[:, i:i + nc] for i in range(WINDOW_CHUNKS + 1)], axis=2)

    kb, vb = band(k), band(v)
    s = jnp.einsum('bnqhgd,bnkhd->bnhgqk', qc, kb).astype(jnp.float32) * (HEAD_DIM ** -0.5)
    n_keys = (WINDOW_CHUNKS + 1) * CHUNK
    key_chunk = jnp.arange(nc)[:, None] - WINDOW_CHUNKS + jnp.arange(n_keys)[None, :] // CHUNK
    valid = (key_chunk >= 0)[None, :, None, None, None, :]
    s = jnp.where(valid, s, -jnp.inf)
    sk = sink.astype(jnp.float32).reshape(1, 1, N_KV_HEADS, grp, 1, 1)
    m = jnp.maximum(jnp.max(s, axis=-1, keepdims=True), sk)
    p = jnp.exp(s - m)
    denom = jnp.sum(p, axis=-1, keepdims=True) + jnp.exp(sk - m)
    p = (p / denom).astype(v.dtype)
    o = jnp.einsum('bnhgqk,bnkhd->bnqhgd', p, vb)
    return o.reshape(B, S, ATTN_WIDTH)

def conformer_conv(a, b, dw, dw_b, ln_g, ln_b, pw):
    g = a * jax.nn.sigmoid(b)
    gp = jnp.pad(g, ((0, 0), (CONV_KERNEL - 1, 0), (0, 0)))
    y = lax.conv_general_dilated(gp, dw[:, None, :], window_strides=(1,), padding='VALID',
                                 dimension_numbers=('NWC', 'WIO', 'NWC'),
                                 feature_group_count=CONV_WIDTH) + dw_b
    y = jax.nn.silu(layer_norm(y, ln_g, ln_b))
    return y @ pw

def setup_inputs(seed: int = 0) -> dict:
    key = jax.random.key(seed)
    ks = jax.random.split(key, 20)
    f32 = jnp.float32

    def nrm(k, shape, scale):
        return jax.random.normal(k, shape, f32) * scale

    L, D = DEPTH, D_MODEL
    return {
        "x": nrm(ks[0], (BATCH, SEQ, D), 1.0),
        "c": nrm(ks[1], (BATCH, D), 1.0),
        "norm_g": 1.0 + nrm(ks[2], (L, D), 0.05),
        "w_ada": nrm(ks[3], (L, D, 3 * D), 0.5 * D ** -0.5),
        "b_ada": nrm(ks[4], (L, 3 * D), 0.01),
        "w_in": nrm(ks[5], (L, D, IN_WIDTH), D ** -0.5),
        "pool_w": nrm(ks[6], (L, N_POOL_GROUPS, POOL_GROUP, POOL_GROUP), POOL_GROUP ** -0.5),
        "pool_scale": 1.0 + nrm(ks[7], (L, POOL_WIDTH), 0.1),
        "attn_sink": nrm(ks[8], (L, N_Q_HEADS), 1.0),
        "conv_dw": nrm(ks[9], (L, CONV_KERNEL, CONV_WIDTH), CONV_KERNEL ** -0.5),
        "conv_dw_b": nrm(ks[10], (L, CONV_WIDTH), 0.01),
        "conv_ln_g": 1.0 + nrm(ks[11], (L, CONV_WIDTH), 0.05),
        "conv_ln_b": nrm(ks[12], (L, CONV_WIDTH), 0.01),
        "conv_pw": nrm(ks[13], (L, CONV_WIDTH, CONV_WIDTH), CONV_WIDTH ** -0.5),
        "w_branch_pool": nrm(ks[14], (L, POOL_WIDTH, D), POOL_WIDTH ** -0.5),
        "w_branch_attn": nrm(ks[15], (L, ATTN_WIDTH, D), ATTN_WIDTH ** -0.5),
        "w_branch_conv": nrm(ks[16], (L, CONV_WIDTH, D), CONV_WIDTH ** -0.5),
        "w_out": nrm(ks[17], (L, D, D), D ** -0.5),
        "final_g": 1.0 + nrm(ks[18], (D,), 0.05),
    }

def reference(x, c, norm_g, w_ada, b_ada, w_in, pool_w, pool_scale, attn_sink, conv_dw, conv_dw_b,
              conv_ln_g, conv_ln_b, conv_pw, w_branch_pool, w_branch_attn, w_branch_conv, w_out,
              final_g):
    B, S, _ = x.shape
    split_idx = np.cumsum(IN_SPLITS)[:-1].tolist()
    c_act = jax.nn.silu(c)
    for l in range(DEPTH):
        mod = c_act @ w_ada[l] + b_ada[l]
        shift, scale, gate = jnp.split(mod, 3, axis=-1)
        h = rms_norm(x, norm_g[l]) * (1 + scale[:, None]) + shift[:, None]
        proj = h @ w_in[l]
        pool_u, pool_z, q, k, v, attn_z, conv_a, conv_b, conv_z, gates = jnp.split(proj, split_idx, axis=-1)
        y_pool = multiscale_pool(pool_u, pool_w[l], pool_scale[l]) * jax.nn.silu(pool_z)
        y_attn = window_attention(q.reshape(B, S, N_Q_HEADS, HEAD_DIM),
                                  k.reshape(B, S, N_KV_HEADS, HEAD_DIM),
                                  v.reshape(B, S, N_KV_HEADS, HEAD_DIM),
                                  attn_sink[l]) * jax.nn.silu(attn_z)
        y_conv = conformer_conv(conv_a, conv_b, conv_dw[l], conv_dw_b[l], conv_ln_g[l], conv_ln_b[l],
                                conv_pw[l]) * jax.nn.silu(conv_z)
        g_pool, g_attn, g_conv = jnp.split(jax.nn.sigmoid(gates), 3, axis=-1)
        merged = (g_pool * (y_pool @ w_branch_pool[l])
                  + g_attn * (y_attn @ w_branch_attn[l])
                  + g_conv * (y_conv @ w_branch_conv[l]))
        x = x + gate[:, None] * (merged @ w_out[l])
    return rms_norm(x, final_g)


_drawn_inputs = setup_inputs


def setup_inputs(seed=0):
    import zlib

    import numpy as np

    out = dict(_drawn_inputs(seed))
    spreads = {}
    factors = {'norm_g': 6.072,
     'b_ada': 8.0,
     'pool_scale': 5.814,
     'attn_sink': 8.0,
     'conv_dw_b': 64.0,
     'conv_ln_g': 49.522,
     'conv_ln_b': 200.0}
    for name, (base, spread) in spreads.items():
        noise = np.random.default_rng([zlib.crc32(name.encode()), seed]).standard_normal(out[name].shape)
        drawn = base * np.exp(spread * noise) if base else spread * noise
        out[name] = __import__('jax').numpy.asarray(drawn.astype(out[name].dtype))
    for name, factor in factors.items():
        out[name] = (out[name] * factor).astype(out[name].dtype)
    return out
```

```python
import concourse.bass as bass
from concourse import mybir
from contextlib import ExitStack

P = 128
D_MODEL, SEQ = 2048, 256
TH = SEQ // P
KT = D_MODEL // P
COLS = 512
PK = 4
RING = 4
EPS = 1e-6
BRANCH = 1024
BT = BRANCH // P
TAPS = 31
HEADS, KV_HEADS, HEAD_DIM = 16, 4, 64
GROUP = HEADS // KV_HEADS
CHUNK = 64
WINDOWS = (2, 4, 8, 16)
PAD = 16
COL_POOL_U, COL_POOL_Z, COL_Q, COL_KV, COL_ATTN_Z = 0, 1024, 2048, 3072, 3584
COL_CONV_A, COL_CONV_B, COL_CONV_Z, COL_GATES = 4608, 5632, 6656, 7680
MASKED = -1e30

V_NORM_G, V_B_ADA, V_POOL_SCALE, V_DW_B, V_LN_G, V_LN_B, V_ROWS = 0, 16, 64, 72, 80, 88, 96

ADA0 = 32
M_CONV, M_POOL, M_KV, M_Q = 0, 16, 24, 28
M_Z, M_ATTN, M_PW, M_POOLB, M_CONVB, M_OUT, M_END = 36, 60, 84, 88, 112, 136, 152
N_ATTN, N_PW, N_POOLB, N_CONVB, N_OUT = 15, 23, 25, 33, 41
CHUNK_END = {n: 4 * n + 4 for n in range(N_ATTN)}
CHUNK_END.update({N_PW + j: M_PW + 2 * j + 2 for j in range(2)})
CHUNK_END.update({N_OUT + j: M_OUT + 4 * j + 4 for j in range(4)})
TAP_STEP = 5
DVE_TILES = 6


def program(nc, a, out):
    F32 = mybir.dt.float32
    F32R = mybir.dt.float32r
    ALU = mybir.AluOpType
    ACT = mybir.ActivationFunctionType
    AX = mybir.AxisListType.X
    HALF = D_MODEL // 2

    base = 16512
    KB = 1024

    def at(name, shape, dt, offset):
        return nc.alloc_sbuf_tensor_at(name, shape, dt, offset=base + offset)

    act_h = at("act_h", [P, KT, SEQ], F32R, 0)
    act_l = at("act_l", [P, KT, SEQ], F32R, 16 * KB)
    wh = at("wh", [P, RING, PK, COLS], F32R, 32 * KB)
    wl = at("wl", [P, RING, PK, COLS], F32R, 64 * KB)
    raw = at("raw", [P, RING, PK, COLS], F32, 96 * KB)
    s0_h = at("s0_h", [P, BT, SEQ], F32R, 128 * KB)
    s0_l = at("s0_l", [P, BT, SEQ], F32R, 136 * KB)
    s1_h = at("s1_h", [P, BT, SEQ], F32R, 144 * KB)
    s1_l = at("s1_l", [P, BT, SEQ], F32R, 152 * KB)
    merged = at("merged", [P, TH, D_MODEL], F32, 160 * KB)
    zs_pool = at("zs_pool", [P, TH, BRANCH], F32, 176 * KB)
    zs_attn = at("zs_attn", [P, TH, BRANCH], F32, 184 * KB)
    zs_conv = at("zs_conv", [P, TH, BRANCH], F32, 192 * KB)
    x_tok = at("x_tok", [P, TH, D_MODEL], F32, 160 * KB)
    x_chan = at("x_chan", [P, KT, SEQ], F32, 144 * KB)
    square_out = at("square_out", [P, D_MODEL], F32, 128 * KB)
    h_tmp = at("h_tmp", [P, PK, SEQ], F32, 136 * KB)
    ada_sums = at("ada_sums", [P, 2, COLS], F32, 176 * KB)
    vec_rows = at("vec_rows", [P, P], F32, 192 * KB)
    tap_rows = at("tap_rows", [P, 2, P], F32, 193 * KB)
    conv_in = at("conv_in", [P, BT, TAPS - 1 + SEQ], F32, 128 * KB)
    k_chan = at("k_chan", [P, KV_HEADS // 2, SEQ], F32, 128 * KB + 9152)
    kv_tok = at("kv_tok", [P, TH, COLS], F32, 128 * KB + 11200)
    pool_in = at("pool_in", [P, BT, PAD + SEQ], F32, 144 * KB)
    win_a = at("win_a", [P, 2, PAD + SEQ], F32, 144 * KB + 8704)
    win_b = at("win_b", [P, 2, PAD + SEQ], F32, 144 * KB + 10880)
    probs = at("probs", [P, GROUP * SEQ], F32, 144 * KB)
    probs_t = at("probs_t", [P, 2, COLS], F32, 148 * KB)
    q_chan = at("q_chan", [P, 2, GROUP, SEQ], F32, 152 * KB)
    conv_acc = at("conv_acc", [P, BT, SEQ], F32, 160 * KB)
    pool_w = at("pool_w", [P, 4, 2, SEQ], F32, 168 * KB)
    pool_silu = at("pool_silu", [P, TH, COLS], F32, 168 * KB)
    squares = at("squares", [P, BT, SEQ], F32, 168 * KB)
    glu_a = at("glu_a", [P, TH, COLS], F32, 184 * KB)
    glu_b = at("glu_b", [P, TH, COLS], F32, 188 * KB)
    q_tok = at("q_tok", [P, TH, COLS], F32, 184 * KB)
    u_tok = at("u_tok", [P, TH, COLS], F32, 192 * KB)
    inv_count = at("inv_count", [P, 4, SEQ], F32, 196 * KB)
    tap_prod = at("tap_prod", [P, 2, SEQ], F32, 192 * KB)
    gate_sig = at("gate_sig", [P, TH, COLS], F32, 184 * KB)
    gated = at("gated", [P, TH, COLS], F32, 192 * KB)
    gate_rows = at("gate_rows", [P, D_MODEL], F32, 176 * KB)
    final_rows = at("final_rows", [P, D_MODEL], F32, 184 * KB)
    x_res = at("x_res", [P, TH, D_MODEL], F32, 144 * KB)
    out_tmp = at("out_tmp", [P, TH, COLS], F32, 192 * KB)
    ident = at("ident", [P, P], F32, 200 * KB)
    ones = at("ones", [P, P], F32, 200 * KB + 512)
    vec = at("vec", [P, V_ROWS], F32, 201 * KB)
    taps = at("taps", [P, TAPS * BT], F32, 201 * KB + 384)
    mask = at("mask", [P, P + SEQ], F32, 201 * KB + 1408)
    gate_sums = at("gate_sums", [P, COLS], F32, 201 * KB + 2944)
    ln_stat = at("ln_stat", [P, SEQ], F32, 201 * KB + 4992)
    small = at("small", [P, 128], F32, 201 * KB + 6016)
    ln_rstd, ln_newton = squares[:, 0, :], squares[:, 1, :]
    square_dump = gate_sums[:, :]
    c_act = small[:, 0:16]
    c_sig = small[:, 16:32]
    sinks = small[:, 32:48]
    x_sum = small[:, 48:50]
    x_rstd = small[:, 50:52]
    mod_scale = small[:, 52:56]
    mod_shift = small[:, 56:60]
    row_max = small[:, 60:64]
    neg_max = small[:, 64:68]
    sink_exp = small[:, 68:72]
    denom = small[:, 72:76]
    inv_den = small[:, 76:80]
    out_sums = small[:, 80:88]
    out_rstd = small[:, 88:90]
    out_sum = small[:, 90:92]
    x_var = small[:, 92:94]
    newton = small[:, 94:96]

    ctx = ExitStack()
    with ctx:
        def bank(name, shape):
            return ctx.enter_context(nc.psum_tensor(name, shape, F32))

        def sem(name):
            return ctx.enter_context(nc.semaphore(name))

        acc = [bank("acc_even", [P, TH, COLS]), bank("acc_odd", [P, TH, COLS])]
        pa = bank("side_a", [P, 2 * COLS])
        pb = bank("side_b", [P, 2 * COLS])

        x_loaded, vec_loaded, tap_loaded = sem("x_loaded"), sem("vec_loaded"), sem("tap_loaded")
        c_loaded, sink_loaded, pool_w_loaded = sem("c_loaded"), sem("sink_loaded"), sem("pool_w_loaded")
        gate_b_loaded, x_res_loaded, final_loaded = sem("gate_b_loaded"), sem("x_res_loaded"), sem("final_loaded")
        stored = sem("stored")
        loaded = [sem(f"loaded_{s}") for s in range(RING)]
        high_done = sem("high_done")
        raw_done = sem("raw_done")
        used = sem("used")
        acc_free = [sem("acc_even_free"), sem("acc_odd_free")]
        pool_chain, dve_chain, act_chain = sem("pool_chain"), sem("dve_chain"), sem("act_chain")
        ident_ready, consts_ready, pads_ready = sem("ident_ready"), sem("consts_ready"), sem("pads_ready")
        counts_ready, inv_ready = sem("counts_ready"), sem("inv_ready")
        vec_t, vec_ready, c_ready = sem("vec_transposed"), sem("vec_ready"), sem("c_ready")
        var_ready, root_ready = sem("var_ready"), sem("root_ready")
        x_squared, x_scaled = sem("x_squared"), sem("x_scaled")
        x_t, x_copied = sem("x_transposed"), sem("x_copied")
        ada_summed, mod_t, mod_ready = sem("ada_summed"), sem("mod_transposed"), sem("mod_ready")
        h_high, h_ready = sem("h_high"), sem("h_ready")
        glu_ready, glu_t, glu_copied = sem("glu_ready"), sem("glu_transposed"), sem("glu_copied")
        conv_dve, conv_pool = sem("conv_dve"), sem("conv_pool")
        ln_summed, ln_centered, ln_squared = sem("ln_summed"), sem("ln_centered"), sem("ln_squared")
        ln_sq_summed, ln_scaled, ln_silu = sem("ln_sq_summed"), sem("ln_scaled"), sem("ln_silu")
        ln_high, ln_ready = sem("ln_high"), sem("ln_ready")
        u_t, u_copied, mixed_ready = sem("u_transposed"), sem("u_copied"), sem("mixed_ready")
        pool_mm, pool_out, pool_z_used = sem("pool_mm"), sem("pool_out"), sem("pool_z_used")
        k_t, k_copied, q_t, q_copied = sem("k_transposed"), sem("k_copied"), sem("q_transposed"), sem("q_copied")
        scores_done, scores_read, max_ready = sem("scores_done"), sem("scores_read"), sem("max_ready")
        exp_done, denom_ready = sem("exp_done"), sem("denom_ready")
        probs_td, probs_copied = sem("probs_transposed"), sem("probs_copied")
        pv_done, attn_ready = sem("pv_done"), sem("attn_ready")
        y_t, y_high, y_ready = sem("y_transposed"), sem("y_high"), sem("y_ready")
        merged_ready = sem("merged_ready")
        gate_summed, gate_rows_mm, gate_added = sem("gate_summed"), sem("gate_rows_mm"), sem("gate_added")
        res_ready, res_squared, out_ready = sem("res_ready"), sem("res_squared"), sem("out_ready")

        block = ctx.enter_context(nc.Block())

        w_in = a["w_in"][0].rearrange("(k p) n -> p k n", p=P)
        w_ada = a["w_ada"][0].rearrange("(p k) n -> p k n", k=KT)
        w_pw = a["conv_pw"][0].rearrange("(k p) n -> p k n", p=P)
        w_out = a["w_out"][0].rearrange("(k p) n -> p k n", p=P)
        w_branch = [a[n][0].rearrange("(k p) n -> p k n", p=P)
                    for n in ("w_branch_pool", "w_branch_attn", "w_branch_conv")]
        x_rows = a["x"][0].rearrange("(h p) n -> p h n", p=P)
        out_rows = out[0].rearrange("(h p) n -> p h n", p=P)
        POOL_B, ATTN_B, CONV_B = 0, 1, 2

        def split_g(m):
            return m + ADA0 + (16 if m >= M_OUT else 0)

        def freed(n):
            return acc_free[n % 2], n // 2 + 1

        ATTN_LOOP = (ATTN_B, M_ATTN, ADA0 + M_ATTN, 12, N_ATTN)
        POOL_LOOP = (POOL_B, M_POOLB, ADA0 + M_POOLB, 16, N_POOLB)
        CONV_LOOP = (CONV_B, M_CONVB, ADA0 + 8 + M_CONVB, 16, N_CONVB)

        @block.sync
        def _(sp):
            def load(w, k0, col, g, slot):
                if g >= RING:
                    sp.wait_ge(raw_done, g + (1 - RING))
                sp.dma_start(raw[:, slot], w[:, k0:k0 + PK, col:col + COLS]).then_inc(loaded[slot], 16)

            def load_chunk(w, col, g, kt=KT):
                for i in range(kt // PK):
                    load(w, PK * i, col, g + i, (g + i) % RING)

            sp.dma_start(c_sig, a["c"][0].rearrange("(p k) -> p k", k=KT)).then_inc(c_loaded, 16)
            sp.dma_start(x_tok[:, :, :], x_rows).then_inc(x_loaded, 16)
            for q in range(KT // PK):
                load_chunk(w_ada, D_MODEL + COLS * q, 8 * q)
                load_chunk(w_ada, COLS * q, 8 * q + 4)
            g = ADA0
            for i in range(2):
                load_chunk(w_in, COL_CONV_A + COLS * i, g + 8 * i)
                load_chunk(w_in, COL_CONV_B + COLS * i, g + 8 * i + 4)
            for i in range(2):
                load_chunk(w_in, COL_POOL_U + COLS * i, g + M_POOL + 4 * i)
            sp.wait_ge(x_t, 4)
            sp.dma_start(pool_w[:, :, :, :], a["pool_w"][0].rearrange("g (k p) n -> p g k n", p=P)).then_inc(pool_w_loaded, 16)
            load_chunk(w_in, COL_KV, g + M_KV)
            for i in range(2):
                load_chunk(w_in, COL_Q + COLS * i, g + M_Q + 4 * i)
            for n, col in enumerate((COL_ATTN_Z, COL_POOL_Z, COL_CONV_Z)):
                for i in range(2):
                    load_chunk(w_in, col + COLS * i, g + M_Z + 8 * n + 4 * i)

            def branch_loads(b, g0, step):
                for it in range(2):
                    shift = it * (2 * COLS)
                    for j in range(2):
                        for i in range(4):
                            k = 6 * j + i
                            load(w_in, PK * i, it * (2 * COLS) + COL_GATES + D_MODEL * b + COLS * j,
                                 it * step + g0 + k, k % RING)
                        for i in range(2):
                            k = 6 * j + 4 + i
                            load(w_branch[b], PK * i, shift + COLS * j, it * step + g0 + k, k % RING)
                    if step == 16:
                        for i in range(4):
                            load(w_ada, PK * i, it * COLS + 2 * D_MODEL + (COLS * 2 if b == CONV_B else 0),
                                 it * step + g0 + 12 + i, i)

            branch_loads(ATTN_B, ADA0 + M_ATTN, 12)
            load_chunk(w_pw, 0, ADA0 + M_PW, BT)
            load_chunk(w_pw, COLS, ADA0 + M_PW + 2, BT)
            sp.wait_ge(y_t, 4)
            sp.dma_start(gate_rows[:, :], a["b_ada"][0:1, 2 * D_MODEL:3 * D_MODEL].partition_broadcast(P)
                         ).then_inc(gate_b_loaded, 16)
            branch_loads(POOL_B, ADA0 + M_POOLB, 16)
            sp.wait_ge(used, M_CONVB)
            sp.dma_start(x_res[:, :, :], x_rows).then_inc(x_res_loaded, 16)
            branch_loads(CONV_B, ADA0 + 8 + M_CONVB, 16)
            for j in range(4):
                load_chunk(w_out, COLS * j, ADA0 + 16 + M_OUT + 4 * j)
                if j == 0:
                    sp.wait_ge(acc_free[(N_OUT - 1) % 2], (N_OUT - 1) // 2 + 1)
                    sp.dma_start(final_rows[:, :], a["final_g"].unsqueeze(0).partition_broadcast(P)
                                 ).then_inc(final_loaded, 16)
            for h in range(TH):
                for half in range(2):
                    sp.wait_ge(out_ready, 2 * h + half + 1)
                    cols = slice(HALF * half, HALF * (half + 1))
                    sp.dma_start(out_rows[:, h, cols], x_res[:, h, cols]).then_inc(stored, 16)
            sp.wait_ge(stored, 16 * 2 * TH)

        @block.gpsimd
        def _(pool):
            count = [0]

            def chained(ins):
                count[0] += 1
                ins.then_inc(pool_chain, 1)
                pool.wait_ge(pool_chain, count[0])

            for row, name, rows in ((V_NORM_G, "norm_g", 16), (V_B_ADA, "b_ada", 48),
                                    (V_POOL_SCALE, "pool_scale", 8), (V_DW_B, "conv_dw_b", 8),
                                    (V_LN_G, "conv_ln_g", 8), (V_LN_B, "conv_ln_b", 8)):
                pool.dma_start(vec_rows[row:row + rows, :], a[name][0].rearrange("(r p) -> r p", p=P)
                               ).then_inc(vec_loaded, 16)
            tap_view = a["conv_dw"][0].rearrange("k (t c) -> (k t) c", c=P)
            for i in range(2):
                pool.dma_start(tap_rows[0:124, i, :], tap_view[124 * i:124 * (i + 1), :]).then_inc(tap_loaded, 16)
            pool.dma_start(sinks, a["attn_sink"][0, :].partition_broadcast(P)).then_inc(sink_loaded, 16)
            chained(nc.gpsimd.memset(ident[:, :], 0.0))
            nc.gpsimd.affine_select(out=ident[:, :], in_=ident[:, :], compare_op=ALU.not_equal, fill=1.0,
                                    base=0, pattern=[[-1, P]], channel_multiplier=1).then_inc(ident_ready, 1)
            nc.gpsimd.iota(inv_count[:, 3, :], pattern=[[1, SEQ]], base=1, channel_multiplier=0,
                           allow_small_or_imprecise_dtypes=True).then_inc(counts_ready, 1)
            nc.gpsimd.memset(ones[:, :], 1.0)
            chained(nc.gpsimd.memset(mask[:, :], 0.0))
            nc.gpsimd.memset(mask[0:CHUNK, CHUNK:P], MASKED)
            nc.gpsimd.memset(mask[0:CHUNK, P + 3 * CHUNK:P + 4 * CHUNK], MASKED)
            nc.gpsimd.memset(mask[CHUNK:P, P:P + CHUNK], MASKED).then_inc(consts_ready, 1)
            pool.wait_ge(h_ready, 4)
            nc.gpsimd.memset(conv_in[:, :, 0:TAPS - 1], 0.0)
            nc.gpsimd.memset(pool_in[:, :, 0:PAD], 0.0).then_inc(pads_ready, 1)
            for i in range(2):
                pool.wait_ge(*freed(2 * i))
                pool.wait_ge(*freed(2 * i + 1))
                nc.gpsimd.tensor_tensor(glu_a[:, :, :], glu_a[:, :, :], glu_b[:, :, :], ALU.mult
                                        ).then_inc(glu_ready, 1)
            pool.wait_ge(inv_ready, 1)
            for i in range(2):
                pool.wait_ge(u_copied, i + 1)
                for g in (2 * i, 2 * i + 1):
                    u = pool_in[:, 2 * g:2 * g + 2, :]
                    src, reach = u, 1
                    for step in range(g + 1):
                        dst = (win_a, win_b)[step % 2]
                        lo = 2 * reach - 1
                        chained(nc.gpsimd.tensor_tensor(dst[:, :, lo:PAD + SEQ], src[:, :, lo:PAD + SEQ],
                                                        src[:, :, lo - reach:PAD + SEQ - reach], ALU.add))
                        src, reach = dst, 2 * reach
                    sums = src[:, :, PAD:PAD + SEQ]
                    chained(nc.gpsimd.tensor_tensor(sums, sums,
                                                    inv_count[:, g:g + 1, :].broadcast_to([P, 2, SEQ]), ALU.mult))
                    tokens = u[:, :, PAD:PAD + SEQ]
                    last = nc.gpsimd.tensor_tensor(tokens, sums, tokens, ALU.subtract)
                    if g == 2 * i:
                        chained(last)
                last.then_inc(mixed_ready, 1)
                pool.wait_ge(mixed_ready, i + 1)
            pool.wait_ge(glu_copied, 2)
            pool.wait_ge(u_t, 2)
            tiles = slice(DVE_TILES, BT)
            width = BT - DVE_TILES

            def wide(column):
                return column.unsqueeze(2).broadcast_to([P, width, SEQ])

            for k in range(TAPS):
                product = tap_prod[:, :, :] if k else conv_acc[:, tiles, :]
                chained(nc.gpsimd.tensor_tensor(product, conv_in[:, tiles, k:k + SEQ],
                                                wide(taps[:, k * BT + DVE_TILES:(k + 1) * BT]), ALU.mult))
                if k:
                    chained(nc.gpsimd.tensor_tensor(conv_acc[:, tiles, :], conv_acc[:, tiles, :], product, ALU.add))
            nc.gpsimd.tensor_tensor(conv_acc[:, tiles, :], conv_acc[:, tiles, :],
                                    wide(vec[:, V_DW_B + DVE_TILES:V_DW_B + BT]), ALU.add).then_inc(conv_pool, 1)

        @block.scalar
        def _(act):
            def split(slot, full, free=None):
                act.wait_ge(loaded[slot], full)
                if free is not None:
                    act.wait_ge(used, free)
                nc.scalar.activation(wh[:, slot], raw[:, slot], ACT.Copy).then_inc(high_done, 1)

            def split_at(m):
                if m < M_END:
                    split(m % RING, 16 * (split_g(m) // RING + 1), m - RING + 1 if m >= RING else None)

            def evacuate(n, dst, func):
                act.wait_ge(used, CHUNK_END[n])
                nc.scalar.activation(dst, acc[n % 2][:, :, :], func).then_inc(acc_free[n % 2], 1)

            def spread(dst, src, ready, count, signal):
                act.wait_ge(ready, count)
                nc.scalar.activation(dst, src, ACT.Copy).then_inc(signal, 1)

            act.wait_ge(c_loaded, 16)
            nc.scalar.activation(c_act, c_sig, ACT.Silu).then_inc(c_ready, 1)
            act.wait_ge(x_loaded, 16)
            for h in range(TH):
                if h:
                    act.wait_ge(x_squared, h)
                nc.scalar.activation(square_out[:, :], x_tok[:, h, :], ACT.Square,
                                     accum_out=x_sum[:, h:h + 1]).then_inc(x_squared, 1)
            act.wait_ge(var_ready, 1)
            nc.scalar.activation(x_rstd, x_var, ACT.Sqrt).then_inc(root_ready, 1)
            for b in range(4):
                act.wait_ge(x_t, b + 1)
                nc.scalar.activation(x_chan[:, 4 * b:4 * b + 4, :],
                                     (pb, pa)[b % 2][:, :].rearrange("p (t s) -> p t s", t=4), ACT.Copy
                                     ).then_inc(x_copied, 1)
            for q in range(4):
                act.wait_ge(mod_ready, q + 1)
                for t in range(PK):
                    k = PK * q + t
                    last = nc.scalar.activation(act_h[:, k, :], x_chan[:, k, :], ACT.Identity,
                                                scale=mod_scale[:, t:t + 1], bias=mod_shift[:, t:t + 1])
                last.then_inc(h_high, 1)
            for m in range(RING):
                split_at(m)

            def softmax_exp(u):
                width = P * (u % 2 + 1)
                act.wait_ge(max_ready, u + 1)
                for g in range(GROUP):
                    cols = slice(g * width, (g + 1) * width)
                    nc.scalar.activation(probs[:, cols], probs[:, cols], ACT.Exp, bias=neg_max[:, g:g + 1],
                                         accum_out=denom[:, g:g + 1])
                nc.scalar.activation(sink_exp, sink_exp, ACT.Exp).then_inc(exp_done, 1)

            for m in range(M_ATTN):
                if m in (3, 11):
                    i = m // 8
                    if i:
                        act.wait_ge(glu_t, i)
                    evacuate(2 * i, glu_a[:, :, :], ACT.Copy)
                if m in (7, 15):
                    evacuate(2 * (m // 8) + 1, glu_b[:, :, :], ACT.Sigmoid)
                if m in (9, 17):
                    i = m // 16
                    if i == 0:
                        act.wait_ge(pads_ready, 1)
                    spread(conv_in[:, 4 * i:4 * i + 4, TAPS - 1:TAPS - 1 + SEQ],
                           (pa, pb)[i][:, :].rearrange("p (t s) -> p t s", t=4), glu_t, i + 1, glu_copied)
                if m in (19, 23):
                    if m == 23:
                        act.wait_ge(u_t, 1)
                    else:
                        act.wait_ge(vec_ready, 1)
                    evacuate(m // 4, u_tok[:, :, :], ACT.Copy)
                if m in (21, 25):
                    i = (m - 21) // 4
                    spread(pool_in[:, 4 * i:4 * i + 4, PAD:PAD + SEQ],
                           (pa, pb)[i][:, :].rearrange("p (t s) -> p t s", t=4), u_t, i + 1, u_copied)
                if m == 27:
                    evacuate(6, kv_tok[:, :, :], ACT.Copy)
                if m == 29:
                    spread(k_chan[:, :, :], pb[:, 0:COLS].rearrange("p (t s) -> p t s", t=2), k_t, 1, k_copied)
                if m in (31, 35):
                    if m == 35:
                        act.wait_ge(q_t, 1)
                    else:
                        act.wait_ge(glu_t, 2)
                    n = m // 4
                    act.wait_ge(used, CHUNK_END[n])
                    for h in range(TH):
                        last = nc.scalar.activation(
                            q_tok[:, h, :].rearrange("p (g k d) -> p k g d", k=2, g=GROUP),
                            acc[n % 2][:, h, :].rearrange("p (k g d) -> p k g d", k=2, g=GROUP), ACT.Copy)
                    last.then_inc(acc_free[n % 2], 1)
                if m in (33, 37):
                    i = (m - 33) // 4
                    if i == 0:
                        act.wait_ge(pool_mm, 2)
                    spread(q_chan[:, i, :, :], (pb, pa)[i][:, :].rearrange("p (t s) -> p t s", t=4),
                           q_t, i + 1, q_copied)
                if m in (39, 43):
                    act.wait_ge(q_t, 2)
                    evacuate(m // 4, zs_attn[:, :, bass.ts((m - 39) // 4, COLS)], ACT.Silu)
                if m in (47, 51):
                    if m == 51:
                        act.wait_ge(pool_z_used, 1)
                    evacuate(m // 4, pool_silu[:, :, :], ACT.Silu)
                if m in (55, 59):
                    act.wait_ge(conv_pool, 1)
                    evacuate(m // 4, zs_conv[:, :, bass.ts((m - 55) // 4, COLS)], ACT.Silu)
                if 38 <= m <= 52 and m % 2 == 0:
                    softmax_exp((m - 38) // 2)
                if 40 <= m <= 54 and m % 2 == 0:
                    u = (m - 40) // 2
                    width = COLS * (u % 2 + 1)
                    act.wait_ge(probs_td, u + 1)
                    nc.scalar.activation(probs_t[:, :, :].rearrange("p k c -> p (k c)")[:, 0:width],
                                         pb[:, 0:width], ACT.Copy).then_inc(probs_copied, 1)
                if m == 54:
                    act.wait_ge(ln_centered, 1)
                    act.wait_ge(pool_z_used, 2)
                    nc.scalar.activation(squares[:, :, :], conv_acc[:, :, :], ACT.Square).then_inc(ln_squared, 1)
                if m == 56:
                    act.wait_ge(var_ready, 2)
                    nc.scalar.activation(ln_rstd, ln_stat[:, :], ACT.Sqrt).then_inc(root_ready, 1)
                    act.wait_ge(ln_scaled, 1)
                    for t in range(BT):
                        last = nc.scalar.activation(squares[:, t, :], conv_acc[:, t, :], ACT.Silu,
                                                    scale=vec[:, V_LN_G + t:V_LN_G + t + 1],
                                                    bias=vec[:, V_LN_B + t:V_LN_B + t + 1])
                    last.then_inc(ln_silu, 1)
                    act.wait_ge(ln_silu, 1)
                    act.wait_ge(attn_ready, 8)
                    nc.scalar.activation(s0_h[:, :, :], squares[:, :, :], ACT.Copy).then_inc(ln_high, 1)
                if m in (57, 58):
                    b = m - 57
                    spread(s1_h[:, 4 * b:4 * b + 4, :], (pb, pa)[b][:, :].rearrange("p (t s) -> p t s", t=4),
                           y_t, b + 1, y_high)
                split_at(m + RING)

            def branch_loop(b, m0, g0, step, n0):
                with act.Fori(0, 2) as it:
                    for k in range(12):
                        if k in (3, 9):
                            n = n0 + 2 * (k // 6)
                            act.wait_ge(used, it * 12 + (m0 + k + 1))
                            act.wait_ge(acc_free[(n - 1) % 2], it * 2 + ((n - 1) // 2 + 1))
                            nc.scalar.activation(gate_sig[:, :, :], acc[n % 2][:, :, :], ACT.Sigmoid
                                                 ).then_inc(acc_free[n % 2], 1)
                        ahead = k + RING + (4 if step == 16 and k + RING >= 12 else 0)
                        split(k % RING, it * (4 * step) + 16 * ((g0 + ahead) // RING + 1),
                              it * 12 + (m0 + k + 1))

            act.wait_ge(y_t, 2)
            branch_loop(*ATTN_LOOP)
            for m in range(M_PW, M_POOLB):
                if m in (84, 85):
                    b = m - 84
                    act.wait_ge(y_t, 3 + b)
                    for t in range(4):
                        last = nc.scalar.activation(s1_h[:, 4 * b + t, :], (pa, pb)[b][:, bass.ts(t, SEQ)], ACT.Copy,
                                                    scale=vec[:, V_POOL_SCALE + 4 * b + t:V_POOL_SCALE + 4 * b + t + 1])
                    last.then_inc(y_high, 1)
                if m == 87:
                    for b in range(2):
                        spread(s0_h[:, 4 * b:4 * b + 4, :], (pa, pb)[b][:, :].rearrange("p (t s) -> p t s", t=4),
                               y_t, 5 + b, y_high)
                split_at(m + RING)
            branch_loop(*POOL_LOOP)
            branch_loop(*CONV_LOOP)
            for j in range(4):
                spread(act_h[:, 4 * j:4 * j + 4, :], (pa, pb)[j % 2][:, :].rearrange("p (t s) -> p t s", t=4),
                       y_t, 7 + j, y_high)

            def square_result(j):
                act.wait_ge(res_ready, j + 1)
                for h in range(TH):
                    if j or h:
                        act.wait_ge(res_squared, TH * j + h)
                    nc.scalar.activation(square_dump, x_res[:, h, bass.ts(j, COLS)], ACT.Square,
                                         accum_out=out_sums[:, 4 * h + j:4 * h + j + 1]).then_inc(res_squared, 1)

            for m in range(M_OUT, M_END):
                if m in (140, 144, 148):
                    square_result((m - 140) // 4)
                split_at(m + RING)
            square_result(3)
            act.wait_ge(var_ready, 3)
            nc.scalar.activation(out_rstd, out_sum, ACT.Sqrt).then_inc(root_ready, 1)

        @block.vector
        def _(dve):
            count = [0]

            def chained(ins):
                count[0] += 1
                ins.then_inc(dve_chain, 1)
                dve.wait_ge(dve_chain, count[0])

            def split(slot, highs):
                dve.wait_ge(high_done, highs)
                nc.vector.tensor_tensor(wl[:, slot], raw[:, slot], wh[:, slot].bitcast(F32), ALU.subtract
                                        ).then_inc(raw_done, 1)

            def split_at(m):
                if m < M_END:
                    split(m % RING, m + 1)

            def low_halves(b, dst_h, dst_l, src):
                dve.wait_ge(y_high, b + 1)
                nc.vector.tensor_tensor(dst_l, src[:, :].rearrange("p (t s) -> p t s", t=4),
                                        dst_h.bitcast(F32), ALU.subtract).then_inc(y_ready, 1)

            def inverse_root(root, var, tmp, number):
                dve.wait_ge(root_ready, number)
                chained(nc.vector.reciprocal(root, root))
                chained(nc.vector.scalar_tensor_tensor(tmp, root, -0.5, root, ALU.mult, ALU.mult))
                chained(nc.vector.tensor_tensor(tmp, tmp, var, ALU.mult))
                chained(nc.vector.scalar_tensor_tensor(root, tmp, 1.5, root, ALU.add, ALU.mult))

            dve.wait_ge(x_squared, 2)
            nc.vector.tensor_scalar(x_var, x_sum, 1.0 / D_MODEL, EPS, ALU.mult, ALU.add).then_inc(var_ready, 1)
            dve.wait_ge(var_ready, 1)
            inverse_root(x_rstd, x_var, newton, 1)
            for h in range(TH):
                last = nc.vector.tensor_scalar(x_tok[:, h, :], x_tok[:, h, :], x_rstd[:, h:h + 1], None, ALU.mult)
            last.then_inc(x_scaled, 1)
            dve.wait_ge(vec_t, 1)
            nc.vector.tensor_copy(vec[:, :], pa[:, 0:V_ROWS])
            last = nc.vector.tensor_copy(taps[:, :].rearrange("p (i r) -> p i r", i=2),
                                         pa[:, 128:640].rearrange("p (i r) -> p i r", i=2)[:, :, 0:124])
            last.then_inc(vec_ready, 1)
            dve.wait_ge(vec_ready, 1)
            scale_b = vec[:, V_B_ADA + KT:V_B_ADA + 2 * KT]
            chained(nc.vector.tensor_scalar(scale_b, scale_b, 1.0, None, ALU.add))
            dve.wait_ge(counts_ready, 1)
            for g in range(4):
                chained(nc.vector.tensor_scalar(inv_count[:, g, :], inv_count[:, 3, :], float(WINDOWS[g]), None, ALU.min))
            last = nc.vector.reciprocal(inv_count[:, :, :], inv_count[:, :, :])
            last.then_inc(inv_ready, 1)

            def ada_piece(sums, slot, full, first):
                dve.wait_ge(loaded[slot], full)
                for i in range(PK):
                    k = PK * slot + i
                    column = c_act[:, k:k + 1]
                    if first and i == 0:
                        last = nc.vector.tensor_scalar(sums, raw[:, slot, i, :], column, None, ALU.mult)
                    else:
                        last = nc.vector.scalar_tensor_tensor(sums, raw[:, slot, i, :], column, sums,
                                                              ALU.mult, ALU.add)
                    if i < PK - 1:
                        chained(last)
                return last

            dve.wait_ge(c_ready, 1)
            for q in range(4):
                if q:
                    dve.wait_ge(mod_t, q)
                    dve.wait_ge(h_ready, q)
                for part in range(2):
                    for i in range(RING):
                        g = 8 * q + 4 * part + i
                        ada_piece(ada_sums[:, part, :], i, 16 * (g // RING + 1), i == 0).then_inc(raw_done, 1)
                        dve.wait_ge(raw_done, g + 1)
                nc.vector.engine_nop().then_inc(ada_summed, 1)
                dve.wait_ge(mod_t, q + 1)
                if q:
                    dve.wait_ge(h_high, q)
                ps = acc[1][:, 0, 8 * q:8 * q + 8]
                k = PK * q
                chained(nc.vector.tensor_tensor(mod_scale, ps[:, 0:4], vec[:, V_B_ADA + KT + k:V_B_ADA + KT + k + 4], ALU.add))
                nc.vector.tensor_tensor(mod_shift, ps[:, 4:8], vec[:, V_B_ADA + k:V_B_ADA + k + 4], ALU.add)
                nc.vector.tensor_tensor(mod_scale, mod_scale, vec[:, V_NORM_G + k:V_NORM_G + k + 4], ALU.mult
                                        ).then_inc(mod_ready, 1)
                dve.wait_ge(mod_ready, q + 1)
                for t in range(PK):
                    last = nc.vector.tensor_scalar(h_tmp[:, t, :], x_chan[:, k + t, :], mod_scale[:, t:t + 1],
                                                   mod_shift[:, t:t + 1], ALU.mult, ALU.add)
                chained(last)
                dve.wait_ge(h_high, q + 1)
                nc.vector.tensor_tensor(act_l[:, k:k + 4, :], h_tmp[:, :, :], act_h[:, k:k + 4, :].bitcast(F32),
                                        ALU.subtract).then_inc(h_ready, 1)
            for m in range(RING):
                split_at(m)

            def conv_tap(i):
                pair, rest = i // (2 * TAPS), i % (2 * TAPS)
                k, t = rest // 2, 2 * pair + rest % 2
                if i == 0:
                    dve.wait_ge(glu_copied, 1)
                if pair == 2 and rest == 0:
                    dve.wait_ge(glu_copied, 2)
                window, tap = conv_in[:, t, k:k + SEQ], taps[:, k * BT + t:k * BT + t + 1]
                if k == 0:
                    ins = nc.vector.tensor_scalar(conv_acc[:, t, :], window, tap,
                                                  vec[:, V_DW_B + t:V_DW_B + t + 1], ALU.mult, ALU.add)
                else:
                    dve.wait_ge(conv_dve, i - 1)
                    ins = nc.vector.scalar_tensor_tensor(conv_acc[:, t, :], window, tap, conv_acc[:, t, :],
                                                         ALU.mult, ALU.add)
                ins.then_inc(conv_dve, 1)

            def score_max(u):
                width = P * (u % 2 + 1)
                scores = pa[:, 0:GROUP * width].rearrange("p (g k) -> p g k", g=GROUP)
                masked = probs[:, 0:GROUP * width].rearrange("p (g k) -> p g k", g=GROUP)
                shown = mask[:, 0:P] if u % 2 == 0 else mask[:, P:P + SEQ]
                sink = sinks[:, GROUP * (u // 2):GROUP * (u // 2) + GROUP]
                dve.wait_ge(scores_done, u + 1)
                if u:
                    dve.wait_ge(probs_td, u)
                else:
                    dve.wait_ge(pool_mm, 2)
                    dve.wait_ge(sink_loaded, 16)
                    dve.wait_ge(consts_ready, 1)
                nc.vector.scalar_tensor_tensor(masked, scores, HEAD_DIM ** -0.5,
                                               shown.unsqueeze(1).broadcast_to([P, GROUP, width]),
                                               ALU.mult, ALU.add).then_inc(scores_read, 1)
                dve.wait_ge(scores_read, u + 1)
                chained(nc.vector.tensor_reduce(row_max, masked, AX, ALU.max))
                chained(nc.vector.tensor_tensor(row_max, row_max, sink, ALU.max))
                nc.vector.tensor_tensor(sink_exp, sink, row_max, ALU.subtract)
                nc.vector.tensor_scalar(neg_max, row_max, -1.0, None, ALU.mult).then_inc(max_ready, 1)

            def denominators(u):
                dve.wait_ge(exp_done, u + 1)
                chained(nc.vector.tensor_tensor(denom, denom, sink_exp, ALU.add))
                nc.vector.reciprocal(inv_den, denom).then_inc(denom_ready, 1)

            def attend(u):
                hkv, h = u // 2, u % 2
                dve.wait_ge(pv_done, u + 1)
                dve.wait_ge(denom_ready, u + 1)
                dve.wait_ge(*freed(9 + hkv // 2))
                for g in range(GROUP):
                    z = zs_attn[:, h, bass.ts(hkv * GROUP + g, HEAD_DIM)]
                    last = nc.vector.scalar_tensor_tensor(z, pb[:, bass.ts(g, HEAD_DIM)], inv_den[:, g:g + 1], z,
                                                          ALU.mult, ALU.mult)
                last.then_inc(attn_ready, 1)

            taps_done = 0
            for m in range(M_ATTN):
                if m in (27, 32):
                    i = m // 32
                    dve.wait_ge(pool_mm, i + 1)
                    nc.vector.tensor_copy(zs_pool[:, :, bass.ts(i, COLS)],
                                          pa[:, :].rearrange("p (h c) -> p h c", h=TH)).then_inc(pool_out, 1)
                if m in (47, 51):
                    i = (m - 47) // 4
                    half = zs_pool[:, :, bass.ts(i, COLS)]
                    dve.wait_ge(*freed(m // 4))
                    dve.wait_ge(pool_out, 2)
                    nc.vector.tensor_tensor(half, half, pool_silu[:, :, :], ALU.mult).then_inc(pool_z_used, 1)
                if 41 <= m <= 55 and m % 2:
                    attend((m - 41) // 2)
                if 38 <= m <= 52 and m % 2 == 0:
                    score_max((m - 38) // 2)
                if 39 <= m <= 53 and m % 2:
                    denominators((m - 39) // 2)
                if 10 <= m:
                    for i in range(taps_done, min(taps_done + TAP_STEP, DVE_TILES * TAPS)):
                        conv_tap(i)
                    taps_done = min(taps_done + TAP_STEP, DVE_TILES * TAPS)
                if m == 54:
                    dve.wait_ge(ln_summed, 1)
                    chained(nc.vector.tensor_scalar(ln_stat[:, :], pa[:, 0:SEQ], 1.0 / BRANCH, None, ALU.mult))
                    nc.vector.tensor_tensor(conv_acc[:, :, :], conv_acc[:, :, :],
                                            ln_stat[:, :].unsqueeze(1).broadcast_to([P, BT, SEQ]), ALU.subtract
                                            ).then_inc(ln_centered, 1)
                if m == 56:
                    dve.wait_ge(ln_sq_summed, 1)
                    nc.vector.tensor_scalar(ln_stat[:, :], pa[:, COLS:COLS + SEQ], 1.0 / BRANCH, EPS,
                                            ALU.mult, ALU.add).then_inc(var_ready, 1)
                    dve.wait_ge(var_ready, 2)
                    inverse_root(ln_rstd, ln_stat[:, :], ln_newton, 2)
                    nc.vector.tensor_tensor(conv_acc[:, :, :], conv_acc[:, :, :],
                                            ln_rstd.unsqueeze(1).broadcast_to([P, BT, SEQ]), ALU.mult
                                            ).then_inc(ln_scaled, 1)
                if m == 57:
                    dve.wait_ge(ln_high, 1)
                    nc.vector.tensor_tensor(s0_l[:, :, :], squares[:, :, :], s0_h[:, :, :].bitcast(F32),
                                            ALU.subtract).then_inc(ln_ready, 1)
                if m in (57, 58):
                    b = m - 57
                    tiles = slice(4 * b, 4 * b + 4)
                    low_halves(b, s1_h[:, tiles, :], s1_l[:, tiles, :], (pb, pa)[b])
                split_at(m + RING)

            def branch_loop(b, m0, g0, step, n0):
                gate0 = 2 if b == CONV_B else 0
                with dve.Fori(0, 2) as it:
                    for k in range(12):
                        if k in (5, 11):
                            n, j = n0 + 2 * (k // 6) + 1, k // 6
                            dve.wait_ge(acc_free[(n - 1) % 2], it * 2 + ((n - 1) // 2 + 1))
                            dve.wait_ge(used, it * 12 + (m0 + k + 1))
                            total = merged[:, :, bass.ds(it * (2 * COLS) + COLS * j, COLS)]
                            if b == ATTN_B:
                                nc.vector.tensor_tensor(total, acc[n % 2][:, :, :], gate_sig[:, :, :], ALU.mult
                                                        ).then_inc(acc_free[n % 2], 1)
                            else:
                                dve.wait_ge(raw_done, it * step + (g0 + k + RING))
                                nc.vector.tensor_tensor(gated[:, :, :], acc[n % 2][:, :, :], gate_sig[:, :, :],
                                                        ALU.mult).then_inc(acc_free[n % 2], 1)
                                dve.wait_ge(acc_free[n % 2], it * 2 + (n // 2 + 1))
                                nc.vector.tensor_tensor(total, total, gated[:, :, :], ALU.add
                                                        ).then_inc(merged_ready, 1)
                        if step == 16 and k == 11:
                            dve.wait_ge(gate_rows_mm, it + (gate0 + 1))
                            dve.wait_ge(gate_b_loaded, 16)
                            row = gate_rows[:, bass.ds(it * COLS + COLS * gate0, COLS)]
                            nc.vector.tensor_tensor(row, row, pa[:, 0:COLS], ALU.add).then_inc(gate_added, 1)
                        split(k % RING, it * 12 + (m0 + k + RING + 1))
                        if step == 16 and k == 7:
                            for i in range(RING):
                                dve.wait_ge(loaded[i], it * (4 * step) + 16 * ((g0 + 12) // RING + 1))
                                for t in range(PK):
                                    column = c_act[:, PK * i + t:PK * i + t + 1]
                                    src = raw[:, i, t, :]
                                    if i == 0 and t == 0:
                                        last = nc.vector.tensor_scalar(gate_sums[:, :], src, column, None, ALU.mult)
                                    else:
                                        if t:
                                            dve.wait_ge(gate_summed, it * 12 + (12 * gate0 + 3 * i + t))
                                        else:
                                            dve.wait_ge(raw_done, it * 16 + (g0 + 12 + i))
                                        last = nc.vector.scalar_tensor_tensor(gate_sums[:, :], src, column,
                                                                              gate_sums[:, :], ALU.mult, ALU.add)
                                    last.then_inc(gate_summed if t < PK - 1 else raw_done, 1)

            branch_loop(*ATTN_LOOP)
            for m in range(M_PW, M_POOLB):
                if m in (84, 85):
                    b = m - 84
                    dve.wait_ge(y_high, 3 + b)
                    for t in range(4):
                        k = 4 * b + t
                        last = nc.vector.scalar_tensor_tensor(s1_l[:, k, :], (pa, pb)[b][:, bass.ts(t, SEQ)],
                                                              vec[:, V_POOL_SCALE + k:V_POOL_SCALE + k + 1],
                                                              s1_h[:, k, :].bitcast(F32), ALU.mult, ALU.subtract)
                    last.then_inc(y_ready, 1)
                if m in (85, 87):
                    j = (m - 85) // 2
                    n = N_PW + j
                    half = zs_conv[:, :, bass.ts(j, COLS)]
                    dve.wait_ge(*freed(13 + j))
                    dve.wait_ge(used, CHUNK_END[n])
                    nc.vector.tensor_tensor(half, acc[n % 2][:, :, :], half, ALU.mult).then_inc(acc_free[n % 2], 1)
                if m == 87:
                    for b in range(2):
                        tiles = slice(4 * b, 4 * b + 4)
                        low_halves(4 + b, s0_h[:, tiles, :], s0_l[:, tiles, :], (pa, pb)[b])
                split_at(m + RING)
            branch_loop(*POOL_LOOP)
            branch_loop(*CONV_LOOP)
            for j in range(4):
                tiles = slice(4 * j, 4 * j + 4)
                low_halves(6 + j, act_h[:, tiles, :], act_l[:, tiles, :], (pa, pb)[j % 2])

            def residual(j):
                n = N_OUT + j
                cols = bass.ts(j, COLS)
                dve.wait_ge(used, CHUNK_END[n])
                if j:
                    dve.wait_ge(res_ready, j)
                nc.vector.tensor_tensor(out_tmp[:, :, :], acc[n % 2][:, :, :],
                                        gate_rows[:, cols].unsqueeze(1).broadcast_to([P, TH, COLS]), ALU.mult
                                        ).then_inc(acc_free[n % 2], 1)
                dve.wait_ge(*freed(n))
                nc.vector.tensor_tensor(x_res[:, :, cols], x_res[:, :, cols], out_tmp[:, :, :], ALU.add
                                        ).then_inc(res_ready, 1)

            dve.wait_ge(gate_added, 4)
            dve.wait_ge(x_res_loaded, 16)
            for m in range(M_OUT, M_END):
                if m % 4 == 3:
                    residual((m - M_OUT) // 4)
                split_at(m + RING)
            dve.wait_ge(res_squared, 4 * TH)
            chained(nc.vector.tensor_reduce(out_sum, out_sums.rearrange("p (h j) -> p h j", h=TH), AX, ALU.add))
            nc.vector.tensor_scalar(out_sum, out_sum, 1.0 / D_MODEL, EPS, ALU.mult, ALU.add).then_inc(var_ready, 1)
            dve.wait_ge(var_ready, 3)
            inverse_root(out_rstd, out_sum, newton, 3)
            dve.wait_ge(final_loaded, 16)
            for h in range(TH):
                for half in range(2):
                    cols = slice(HALF * half, HALF * (half + 1))
                    nc.vector.scalar_tensor_tensor(x_res[:, h, cols], x_res[:, h, cols], out_rstd[:, h:h + 1],
                                                   final_rows[:, cols], ALU.mult, ALU.mult).then_inc(out_ready, 1)

        @block.tensor
        def _(pe):
            def piece(lhs_h, lhs_l, k0, slot, sums, count, first, last):
                pe.wait_ge(raw_done, count)
                for i in range(PK):
                    for h in range(TH):
                        tokens = slice(P * h, P * (h + 1))
                        begin, end = first and i == 0, last and i == PK - 1
                        xh, xl = lhs_h[:, k0 + i, tokens], lhs_l[:, k0 + i, tokens]
                        nc.tensor.matmul(sums[:, h, :], xh, wh[:, slot, i, :], start=begin, stop=False)
                        nc.tensor.matmul(sums[:, h, :], xh, wl[:, slot, i, :], start=False, stop=False)
                        ins = nc.tensor.matmul(sums[:, h, :], xl, wh[:, slot, i, :], start=False, stop=end)
                ins.then_inc(used, 1)

            def transpose4(dst, src, ready):
                for t in range(4):
                    for h in range(TH):
                        ins = nc.tensor.transpose(dst[:, SEQ * t + P * h:SEQ * t + P * (h + 1)],
                                                  src(h, t), ident[:, :])
                ins.then_inc(ready, 1)

            def block_of(buf, col=0):
                return lambda h, t: buf[:, h, col + P * t:col + P * (t + 1)]

            pe.wait_ge(ident_ready, 1)
            pe.wait_ge(vec_loaded, 16 * 6)
            pe.wait_ge(tap_loaded, 16 * 2)
            nc.tensor.transpose(pa[:, 0:V_ROWS], vec_rows[0:V_ROWS, :], ident[0:V_ROWS, 0:V_ROWS])
            nc.tensor.transpose(pa[:, 128:252], tap_rows[0:124, 0, :], ident[0:124, 0:124])
            nc.tensor.transpose(pa[:, 384:508], tap_rows[0:124, 1, :], ident[0:124, 0:124]).then_inc(vec_t, 1)
            pe.wait_ge(x_scaled, 1)
            for b in range(4):
                if b == 1:
                    pe.wait_ge(vec_ready, 1)
                if b >= 2:
                    pe.wait_ge(x_copied, b - 1)
                transpose4((pb, pa)[b % 2], block_of(x_tok, COLS * b), x_t)
            pe.wait_ge(consts_ready, 1)
            for q in range(4):
                pe.wait_ge(ada_summed, q + 1)
                for part in range(2):
                    for t in range(PK):
                        col = 8 * q + 4 * part + t
                        ins = nc.tensor.matmul(acc[1][:, 0, col:col + 1], ada_sums[:, part, P * t:P * (t + 1)],
                                               ones[:, 0:1], start=True, stop=True)
                ins.then_inc(mod_t, 1)
            pe.wait_ge(h_ready, 4)

            def stream(m, lhs, k0, n, first, last):
                if first and n >= 2:
                    pe.wait_ge(acc_free[n % 2], n // 2)
                piece(*lhs, k0, m % RING, acc[n % 2], split_g(m) + 1, first, last)

            hidden = (act_h, act_l)
            slot0, slot1 = (s0_h, s0_l), (s1_h, s1_l)

            def unit_scores(u):
                hkv, h = u // 2, u % 2
                rows = slice(HEAD_DIM * (hkv % 2), HEAD_DIM * (hkv % 2 + 1))
                width = P * (h + 1)
                if u:
                    pe.wait_ge(scores_read, u)
                pe.wait_ge(q_copied, 2)
                pe.wait_ge(k_copied, 1)
                for g in range(GROUP):
                    ins = nc.tensor.matmul(pa[:, g * width:(g + 1) * width],
                                           q_chan[rows, hkv // 2, g, P * h:P * (h + 1)],
                                           k_chan[rows, hkv // 2, 0:width], start=True, stop=True)
                ins.then_inc(scores_done, 1)

            def unit_transpose(u):
                h = u % 2
                width = P * (h + 1)
                pe.wait_ge(exp_done, u + 1)
                if u:
                    pe.wait_ge(attn_ready, u)
                for kt in range(h + 1):
                    for g in range(GROUP):
                        ins = nc.tensor.transpose(pb[:, COLS * kt + P * g:COLS * kt + P * (g + 1)],
                                                  probs[:, g * width + P * kt:g * width + P * (kt + 1)], ident[:, :])
                ins.then_inc(probs_td, 1)

            def unit_values(u):
                hkv, h = u // 2, u % 2
                pe.wait_ge(probs_copied, u + 1)
                for g in range(GROUP):
                    for kt in range(h + 1):
                        ins = nc.tensor.matmul(pb[:, HEAD_DIM * g:HEAD_DIM * (g + 1)], probs_t[:, kt, P * g:P * (g + 1)],
                                               kv_tok[:, kt, SEQ + HEAD_DIM * hkv:SEQ + HEAD_DIM * (hkv + 1)],
                                               start=(kt == 0), stop=(kt == h))
                ins.then_inc(pv_done, 1)

            def column_sums(dst, src, ready):
                for t in range(BT):
                    ins = nc.tensor.matmul(dst, ones[:, :], src[:, t, :], start=(t == 0), stop=(t == BT - 1))
                ins.then_inc(ready, 1)

            for m in range(M_ATTN):
                n = m // 4
                stream(m, hidden, PK * (m % 4), n, m % 4 == 0, m % 4 == 3)
                if m in (9, 17):
                    i = m // 16
                    pe.wait_ge(glu_ready, i + 1)
                    transpose4((pa, pb)[i], block_of(glu_a), glu_t)
                if m in (21, 25):
                    i = (m - 21) // 4
                    pe.wait_ge(*freed(4 + i))
                    pe.wait_ge(glu_copied, i + 1)
                    transpose4((pa, pb)[i], block_of(u_tok), u_t)
                if m in (27, 32):
                    i = m // 32
                    pe.wait_ge(mixed_ready, i + 1)
                    pe.wait_ge(pool_w_loaded, 16)
                    pe.wait_ge(u_copied, 1)
                    if i:
                        pe.wait_ge(pool_out, 1)
                    for h in range(TH):
                        for gg in range(2):
                            g = 2 * i + gg
                            for k in range(2):
                                lo = PAD + P * h
                                ins = nc.tensor.matmul(pa[:, COLS * h + SEQ * gg:COLS * h + SEQ * (gg + 1)],
                                                       pool_in[:, 2 * g + k, lo:lo + P], pool_w[:, g, k, :],
                                                       start=(k == 0), stop=(k == 1))
                    ins.then_inc(pool_mm, 1)
                if m == 29:
                    pe.wait_ge(*freed(6))
                    pe.wait_ge(u_copied, 2)
                    for t in range(2):
                        for h in range(TH):
                            ins = nc.tensor.transpose(pb[:, SEQ * t + P * h:SEQ * t + P * (h + 1)],
                                                      kv_tok[:, h, P * t:P * (t + 1)], ident[:, :])
                    ins.then_inc(k_t, 1)
                if m in (33, 37):
                    i = (m - 33) // 4
                    pe.wait_ge(*freed(7 + i))
                    if i:
                        pe.wait_ge(pool_out, 2)
                    else:
                        pe.wait_ge(k_copied, 1)
                    transpose4((pb, pa)[i], block_of(q_tok), q_t)
                if 40 <= m <= 54 and m % 2 == 0:
                    unit_transpose((m - 40) // 2)
                if 38 <= m <= 52 and m % 2 == 0:
                    unit_scores((m - 38) // 2)
                if 41 <= m <= 55 and m % 2:
                    unit_values((m - 41) // 2)
                if m == 53:
                    pe.wait_ge(conv_dve, DVE_TILES * TAPS)
                    pe.wait_ge(conv_pool, 1)
                    pe.wait_ge(scores_read, 8)
                    column_sums(pa[:, 0:SEQ], conv_acc, ln_summed)
                if m == 55:
                    pe.wait_ge(ln_squared, 1)
                    column_sums(pa[:, COLS:COLS + SEQ], squares, ln_sq_summed)
                if m in (57, 58):
                    b = m - 57
                    pe.wait_ge(attn_ready, 8)
                    if b:
                        pe.wait_ge(ln_scaled, 1)
                    transpose4((pb, pa)[b], block_of(zs_attn, COLS * b), y_t)

            def branch_loop(b, m0, g0, step, n0, lhs):
                with pe.Fori(0, 2) as it:
                    for k in range(12):
                        n = n0 + 2 * (k // 6) + (k % 6 >= 4)
                        first, last = k % 6 in (0, 4), k % 6 in (3, 5)
                        if first:
                            pe.wait_ge(acc_free[n % 2], it * 2 + n // 2)
                        left, k0 = (hidden, PK * (k % 6)) if k % 6 < 4 else (lhs, PK * (k % 6 - 4))
                        piece(*left, k0, k % RING, acc[n % 2], it * step + (g0 + k + 1), first, last)
                    if step == 16:
                        pe.wait_ge(raw_done, it * 16 + (g0 + 16))
                        nc.tensor.matmul(pa[:, 0:COLS], ones[:, :], gate_sums[:, :], start=True, stop=True
                                         ).then_inc(gate_rows_mm, 1)

            pe.wait_ge(y_ready, 2)
            branch_loop(*ATTN_LOOP, slot1)
            pe.wait_ge(ln_ready, 1)
            for m in range(M_PW, M_POOLB):
                j, i = (m - M_PW) // 2, (m - M_PW) % 2
                stream(m, slot0, PK * i, N_PW + j, i == 0, i == 1)
                if m in (84, 85):
                    b = m - 84
                    pe.wait_ge(pool_z_used, 2)
                    if b == 0:
                        pe.wait_ge(y_ready, 2)
                    transpose4((pa, pb)[b], block_of(zs_pool, COLS * b), y_t)
            for b in range(2):
                pe.wait_ge(*freed(N_PW + b))
                pe.wait_ge(y_ready, 3 + b)
                transpose4((pa, pb)[b], block_of(zs_conv, COLS * b), y_t)
            pe.wait_ge(y_ready, 5)
            branch_loop(*POOL_LOOP, slot1)
            pe.wait_ge(y_ready, 6)
            branch_loop(*CONV_LOOP, slot0)
            pe.wait_ge(merged_ready, 8)

            def merged_by_channels(j):
                if j == 0:
                    pe.wait_ge(gate_added, 4)
                else:
                    pe.wait_ge(y_ready, 5 + j)
                transpose4((pa, pb)[j % 2], block_of(merged, COLS * j), y_t)

            merged_by_channels(0)
            merged_by_channels(1)
            for m in range(M_OUT, M_END):
                j, i = (m - M_OUT) // 4, (m - M_OUT) % 4
                if j == 0:
                    pe.wait_ge(y_ready, 7 + i)
                stream(m, hidden, PK * i, N_OUT + j, i == 0, i == 3)
                if m in (M_OUT, M_OUT + 1):
                    merged_by_channels(2 + m - M_OUT)


_INPUTS = ["x", "c", "norm_g", "w_ada", "b_ada", "w_in", "pool_w", "pool_scale", "attn_sink", "conv_dw",
           "conv_dw_b", "conv_ln_g", "conv_ln_b", "conv_pw", "w_branch_pool", "w_branch_attn",
           "w_branch_conv", "w_out", "final_g"]


def kernel(**inputs):
    import numpy as np
    import concourse.bacc as bacc
    from concourse.bass_utils import run_bass_kernel_spmd as run

    nc = bacc.Bacc("TRN2", target_bir_lowering=False, num_devices=1)
    arrays, args = {}, {}
    for name in _INPUTS:
        array = np.ascontiguousarray(inputs[name])
        arrays[f"in_{name}"] = array
        args[name] = nc.dram_tensor(f"in_{name}", array.shape, mybir.dt.from_np(array.dtype),
                                    kind="ExternalInput").ap()
    out = nc.dram_tensor("out", (1, SEQ, D_MODEL), mybir.dt.float32, kind="ExternalOutput").ap()
    program(nc, args, out)
    result = run(nc, [arrays], core_ids=[0])
    return result.results[0]["out"]
```

```python
import concourse.bass as bass
from concourse import mybir
from contextlib import ExitStack

P = 128
D_MODEL, SEQ = 2048, 256
TH = SEQ // P
KT = D_MODEL // P
COLS = 512
PK = 4
RING = 4
EPS = 1e-6
BRANCH = 1024
BT = BRANCH // P
TAPS = 31
HEADS, KV_HEADS, HEAD_DIM = 16, 4, 64
GROUP = HEADS // KV_HEADS
CHUNK = 64
WINDOWS = (2, 4, 8, 16)
PAD = 16
COL_POOL_U, COL_POOL_Z, COL_Q, COL_KV, COL_ATTN_Z = 0, 1024, 2048, 3072, 3584
COL_CONV_A, COL_CONV_B, COL_CONV_Z, COL_GATES = 4608, 5632, 6656, 7680
MASKED = -1e30

V_NORM_G, V_B_ADA, V_POOL_SCALE, V_DW_B, V_LN_G, V_LN_B, V_ROWS = 0, 16, 64, 72, 80, 88, 96

ADA0 = 32
OPENING = 12
M_CONV, M_POOL, M_KV, M_Q = 0, 16, 24, 28
M_Z, M_ATTN, M_PW, M_POOLB, M_CONVB, M_OUT, M_END = 36, 60, 84, 88, 112, 136, 152
N_ATTN, N_PW, N_POOLB, N_CONVB, N_OUT = 14, 22, 24, 32, 40
CHUNK_END = {0: 10, 1: 11}
CHUNK_END.update({n: 4 * n + 8 for n in range(2, N_ATTN)})
CHUNK_END.update({N_PW + j: M_PW + 2 * j + 2 for j in range(2)})
CHUNK_END.update({N_OUT + j: M_OUT + 4 * j + 4 for j in range(3)})

OPEN = []
for _q in range(4):
    for _i in range(RING):
        if _q and _i == RING - 1:
            OPEN += [("weights", _q - 1, 0)]
        OPEN += [("shift", _q, _i), ("scale", _q, _i)]
    if _q:
        OPEN += [("weights", _q - 1, 1), ("weights", _q - 1, 2)]
OPEN += [("weights", 3, _c) for _c in range(3)]
GATE_AFTER = (3, 6, 9, 11)
SHIFTS = 16


def opening_places(kind):
    return [g for g, piece in enumerate(OPEN) if piece[0] == kind]


def freeing(g):
    if g < len(OPEN) and OPEN[g][0] == "shift":
        return "PE", opening_places("shift").index(g) + 1
    if g < len(OPEN):
        return "DVE", sum(piece[0] != "shift" for piece in OPEN[:g + 1])
    return "DVE", g + 1 - SHIFTS


TAP_STEP = 5
DVE_TILES = 6


def program(nc, a, out):
    F32 = mybir.dt.float32
    F32R = mybir.dt.float32r
    ALU = mybir.AluOpType
    ACT = mybir.ActivationFunctionType
    AX = mybir.AxisListType.X
    HALF = D_MODEL // 2

    base = 16512
    KB = 1024

    def at(name, shape, dt, offset):
        return nc.alloc_sbuf_tensor_at(name, shape, dt, offset=base + offset)

    act_h = at("act_h", [P, KT, SEQ], F32R, 0)
    act_l = at("act_l", [P, KT, SEQ], F32R, 16 * KB)
    wh = at("wh", [P, RING, PK, COLS], F32R, 32 * KB)
    wl = at("wl", [P, RING, PK, COLS], F32R, 64 * KB)
    raw = at("raw", [P, RING, PK, COLS], F32, 96 * KB)
    s0_h = at("s0_h", [P, BT, SEQ], F32R, 128 * KB)
    s0_l = at("s0_l", [P, BT, SEQ], F32R, 136 * KB)
    s1_h = at("s1_h", [P, BT, SEQ], F32R, 144 * KB)
    s1_l = at("s1_l", [P, BT, SEQ], F32R, 152 * KB)
    merged = at("merged", [P, TH, D_MODEL], F32, 160 * KB)
    zs_pool = at("zs_pool", [P, TH, BRANCH], F32, 176 * KB)
    zs_attn = at("zs_attn", [P, TH, BRANCH], F32, 184 * KB)
    zs_conv = at("zs_conv", [P, TH, BRANCH], F32, 192 * KB)
    x_tok = at("x_tok", [P, TH, D_MODEL], F32, 160 * KB)
    x_chan = at("x_chan", [P, KT, SEQ], F32, 144 * KB)
    square_out = at("square_out", [P, D_MODEL], F32, 128 * KB)
    h_tmp = at("h_tmp", [P, PK, SEQ], F32, 136 * KB)
    ada_sums = at("ada_sums", [P, COLS], F32, 176 * KB)
    shift_row = at("shift_row", [1, COLS], F32, 178 * KB)
    vec_rows = at("vec_rows", [P, P], F32, 192 * KB)
    tap_rows = at("tap_rows", [P, 2, P], F32, 193 * KB)
    conv_in = at("conv_in", [P, BT, TAPS - 1 + SEQ], F32, 128 * KB)
    k_chan = at("k_chan", [P, KV_HEADS // 2, SEQ], F32, 128 * KB + 9152)
    kv_tok = at("kv_tok", [P, TH, COLS], F32, 128 * KB + 11200)
    pool_in = at("pool_in", [P, BT, PAD + SEQ], F32, 144 * KB)
    win_a = at("win_a", [P, 2, PAD + SEQ], F32, 144 * KB + 8704)
    win_b = at("win_b", [P, 2, PAD + SEQ], F32, 144 * KB + 10880)
    probs = at("probs", [P, GROUP * SEQ], F32, 144 * KB)
    probs_t = at("probs_t", [P, 2, COLS], F32, 148 * KB)
    q_chan = at("q_chan", [P, 2, GROUP, SEQ], F32, 152 * KB)
    conv_acc = at("conv_acc", [P, BT, SEQ], F32, 160 * KB)
    pool_w = at("pool_w", [P, 4, 2, SEQ], F32, 168 * KB)
    pool_silu = at("pool_silu", [P, TH, COLS], F32, 168 * KB)
    squares = at("squares", [P, BT, SEQ], F32, 168 * KB)
    glu_a = [at("glu_a0", [P, TH, COLS], F32, 184 * KB), at("glu_a1", [P, TH, COLS], F32, 192 * KB)]
    glu_b = at("glu_b", [P, TH, COLS], F32, 188 * KB)
    q_tok = at("q_tok", [P, TH, COLS], F32, 184 * KB)
    u_tok = at("u_tok", [P, TH, COLS], F32, 192 * KB)
    inv_count = at("inv_count", [P, 4, SEQ], F32, 196 * KB)
    tap_prod = at("tap_prod", [P, 2, SEQ], F32, 192 * KB)
    gate_sig = at("gate_sig", [P, TH, COLS], F32, 184 * KB)
    gated = at("gated", [P, TH, COLS], F32, 188 * KB)
    gate_rows = at("gate_rows", [P, D_MODEL], F32, 176 * KB)
    final_rows = at("final_rows", [P, D_MODEL], F32, 184 * KB)
    x_res = at("x_res", [P, TH, D_MODEL], F32, 144 * KB)
    out_tmp = at("out_tmp", [P, TH, COLS], F32, 192 * KB)
    ident = at("ident", [P, P], F32, 200 * KB)
    ones = at("ones", [P, P], F32, 200 * KB + 512)
    vec = at("vec", [P, V_ROWS], F32, 201 * KB)
    taps = at("taps", [P, TAPS * BT], F32, 201 * KB + 384)
    mask = at("mask", [P, P + SEQ], F32, 201 * KB + 1408)
    gate_sums = at("gate_sums", [P, COLS], F32, 201 * KB + 2944)
    ln_stat = at("ln_stat", [P, SEQ], F32, 201 * KB + 4992)
    small = at("small", [P, 128], F32, 201 * KB + 6016)
    ln_rstd, ln_newton = squares[:, 0, :], squares[:, 1, :]
    square_dump = gate_sums[:, :]
    c_act = small[:, 0:16]
    c_in = small[:, 16:32]
    sinks = small[:, 32:48]
    x_sum = small[:, 48:50]
    x_rstd = small[:, 50:52]
    mod_scale = small[:, 52:56]
    mod_shift = small[:, 56:60]
    row_max = small[:, 60:64]
    neg_max = small[:, 64:68]
    sink_exp = small[:, 68:72]
    denom = small[:, 72:76]
    inv_den = small[:, 76:80]
    out_sums = small[:, 80:88]
    out_rstd = small[:, 88:90]
    out_sum = small[:, 90:92]
    x_var = small[:, 92:94]
    newton = small[:, 94:96]

    ctx = ExitStack()
    with ctx:
        def bank(name, shape):
            return ctx.enter_context(nc.psum_tensor(name, shape, F32))

        def sem(name):
            return ctx.enter_context(nc.semaphore(name))

        acc = [bank("acc_even", [P, TH, COLS]), bank("acc_odd", [P, TH, COLS])]
        pa = bank("side_a", [P, 2 * COLS])
        pb = bank("side_b", [P, 2 * COLS])

        x_loaded, vec_loaded, tap_loaded = sem("x_loaded"), sem("vec_loaded"), sem("tap_loaded")
        c_loaded, sink_loaded, pool_w_loaded = sem("c_loaded"), sem("sink_loaded"), sem("pool_w_loaded")
        gate_b_loaded, x_res_loaded, final_loaded = sem("gate_b_loaded"), sem("x_res_loaded"), sem("final_loaded")
        stored = sem("stored")
        loaded = [sem(f"loaded_{s}") for s in range(RING)]
        high_done = sem("high_done")
        raw_done = sem("raw_done")
        shift_done = sem("shift_done")
        used = sem("used")
        acc_free = [sem("acc_even_free"), sem("acc_odd_free")]
        pool_chain, dve_chain = sem("pool_chain"), sem("dve_chain")
        ident_ready, consts_ready, pads_ready = sem("ident_ready"), sem("consts_ready"), sem("pads_ready")
        counts_ready, inv_ready = sem("counts_ready"), sem("inv_ready")
        vec_t, vec_ready, c_ready = sem("vec_transposed"), sem("vec_ready"), sem("c_ready")
        var_ready, root_ready = sem("var_ready"), sem("root_ready")
        x_squared, x_scaled = sem("x_squared"), sem("x_scaled")
        x_t, x_copied = sem("x_transposed"), sem("x_copied")
        shift_copied = sem("shift_copied")
        mod_t, mod_ready = sem("mod_transposed"), sem("mod_ready")
        h_high, h_ready = sem("h_high"), sem("h_ready")
        a1_copied = sem("a1_copied")
        glu_ready, glu_t, glu_copied = sem("glu_ready"), sem("glu_transposed"), sem("glu_copied")
        conv_dve, conv_pool = sem("conv_dve"), sem("conv_pool")
        ln_partial = sem("ln_partial")
        ln_summed, ln_centered, ln_squared = sem("ln_summed"), sem("ln_centered"), sem("ln_squared")
        ln_sq_summed, ln_scaled, ln_silu = sem("ln_sq_summed"), sem("ln_scaled"), sem("ln_silu")
        ln_high, ln_ready = sem("ln_high"), sem("ln_ready")
        u_t, u_copied, mixed_ready = sem("u_transposed"), sem("u_copied"), sem("mixed_ready")
        pool_mm, pool_out, pool_z_used = sem("pool_mm"), sem("pool_out"), sem("pool_z_used")
        k_t, k_copied, q_t, q_copied = sem("k_transposed"), sem("k_copied"), sem("q_transposed"), sem("q_copied")
        scores_done, scores_read, max_ready = sem("scores_done"), sem("scores_read"), sem("max_ready")
        exp_done, denom_ready = sem("exp_done"), sem("denom_ready")
        probs_td, probs_copied = sem("probs_transposed"), sem("probs_copied")
        pv_done, attn_ready = sem("pv_done"), sem("attn_ready")
        y_t, y_high, y_ready = sem("y_transposed"), sem("y_high"), sem("y_ready")
        merged_ready = sem("merged_ready")
        gate_summed, gate_rows_mm, gate_added = sem("gate_summed"), sem("gate_rows_mm"), sem("gate_added")
        res_ready, res_squared = sem("res_ready"), sem("res_squared")
        tile_summed, rstd_ready = sem("tile_summed"), sem("rstd_ready")
        out_ready, out_high = sem("out_ready"), sem("out_high_half_ready")

        block = ctx.enter_context(nc.Block())

        w_in = a["w_in"][0].rearrange("(k p) n -> p k n", p=P)
        w_ada = a["w_ada"][0].rearrange("(p k) n -> p k n", k=KT)
        w_pw = a["conv_pw"][0].rearrange("(k p) n -> p k n", p=P)
        w_out = a["w_out"][0].rearrange("(k p) n -> p k n", p=P)
        w_branch = [a[n][0].rearrange("(k p) n -> p k n", p=P)
                    for n in ("w_branch_pool", "w_branch_attn", "w_branch_conv")]
        x_rows = a["x"][0].rearrange("(h p) n -> p h n", p=P)
        out_rows = out[0].rearrange("(h p) n -> p h n", p=P)
        POOL_B, ATTN_B, CONV_B = 0, 1, 2

        def split_g(m):
            if m < OPENING:
                return opening_places("weights")[m]
            return m + ADA0 + (16 if m >= M_OUT else 0)

        def chunk_of(m):
            return m // 4 - 1

        def freed(n):
            return acc_free[n % 2], n // 2 + 1

        def x_side(b):
            return acc[b % 2][:, :, :].rearrange("p h (t s) -> p (h t) s", s=SEQ)

        def place(k, step):
            return k + (sum(k > before for before in GATE_AFTER) if step == 16 else 0)

        ATTN_LOOP = (ATTN_B, M_ATTN, ADA0 + M_ATTN, 12, N_ATTN)
        POOL_LOOP = (POOL_B, M_POOLB, ADA0 + M_POOLB, 16, N_POOLB)
        CONV_LOOP = (CONV_B, M_CONVB, ADA0 + 8 + M_CONVB, 16, N_CONVB)

        @block.sync
        def _(sp):
            def load(w, k0, col, g):
                if g >= RING:
                    who, count = freeing(g - RING)
                    sp.wait_ge(shift_done if who == "PE" else raw_done, count)
                sp.dma_start(raw[:, g % RING], w[:, k0:k0 + PK, col:col + COLS]).then_inc(loaded[g % RING], 16)

            def load_chunk(w, col, g, kt=KT):
                for i in range(kt // PK):
                    load(w, PK * i, col, g + i)

            sp.dma_start(c_in, a["c"][0].rearrange("(p k) -> p k", k=KT)).then_inc(c_loaded, 16)
            sp.dma_start(x_tok[:, :, :], x_rows).then_inc(x_loaded, 16)
            for g, (kind, q, i) in enumerate(OPEN):
                if kind == "weights":
                    load(w_in, PK * q, (COL_CONV_A, COL_CONV_B, COL_CONV_A + COLS)[i], g)
                else:
                    load(w_ada, PK * i, (D_MODEL if kind == "scale" else 0) + COLS * q, g)
            g = ADA0
            load_chunk(w_in, COL_CONV_B + COLS, g + OPENING)
            for i in range(2):
                load_chunk(w_in, COL_POOL_U + COLS * i, g + M_POOL + 4 * i)
            load_chunk(w_in, COL_KV, g + M_KV)
            for i in range(2):
                load_chunk(w_in, COL_Q + COLS * i, g + M_Q + 4 * i)
            for n, col in enumerate((COL_ATTN_Z, COL_POOL_Z, COL_CONV_Z)):
                for i in range(2):
                    load_chunk(w_in, col + COLS * i, g + M_Z + 8 * n + 4 * i)

            def branch_loads(b, g0, step):
                for it in range(2):
                    for k in range(12):
                        g = it * step + g0 + place(k, step)
                        col = 2 * COLS * it + COLS * (k // 6)
                        if k % 6 < 4:
                            load(w_in, PK * (k % 6), COL_GATES + D_MODEL * b + col, g)
                        else:
                            load(w_branch[b], PK * (k % 6 - 4), col, g)
                        if step == 16 and k in GATE_AFTER:
                            load(w_ada, PK * GATE_AFTER.index(k),
                                 it * COLS + 2 * D_MODEL + (COLS * 2 if b == CONV_B else 0), g + 1)

            branch_loads(ATTN_B, ADA0 + M_ATTN, 12)
            load_chunk(w_pw, 0, ADA0 + M_PW, BT)
            load_chunk(w_pw, COLS, ADA0 + M_PW + 2, BT)
            branch_loads(POOL_B, ADA0 + M_POOLB, 16)
            branch_loads(CONV_B, ADA0 + 8 + M_CONVB, 16)
            for j in range(4):
                load_chunk(w_out, COLS * j, ADA0 + 16 + M_OUT + 4 * j)
            for h in range(TH):
                sp.wait_ge(out_ready, h + 1)
                sp.dma_start(out_rows[:, h, 0:HALF], x_res[:, h, 0:HALF]).then_inc(stored, 16)
            sp.wait_ge(stored, 16 * 2 * TH)

        @block.gpsimd
        def _(pool):
            count = [0]

            def chained(ins):
                count[0] += 1
                ins.then_inc(pool_chain, 1)
                pool.wait_ge(pool_chain, count[0])

            chained(nc.gpsimd.memset(ident[:, :], 0.0))
            nc.gpsimd.affine_select(out=ident[:, :], in_=ident[:, :], compare_op=ALU.not_equal, fill=1.0,
                                    base=0, pattern=[[-1, P]], channel_multiplier=1).then_inc(ident_ready, 1)
            for row, name, rows in ((V_NORM_G, "norm_g", 16), (V_B_ADA, "b_ada", 48),
                                    (V_POOL_SCALE, "pool_scale", 8), (V_DW_B, "conv_dw_b", 8),
                                    (V_LN_G, "conv_ln_g", 8), (V_LN_B, "conv_ln_b", 8)):
                pool.dma_start(vec_rows[row:row + rows, :], a[name][0].rearrange("(r p) -> r p", p=P)
                               ).then_inc(vec_loaded, 16)
            tap_view = a["conv_dw"][0].rearrange("k (t c) -> (k t) c", c=P)
            for i in range(2):
                pool.dma_start(tap_rows[0:124, i, :], tap_view[124 * i:124 * (i + 1), :]).then_inc(tap_loaded, 16)
            pool.dma_start(sinks, a["attn_sink"][0, :].partition_broadcast(P)).then_inc(sink_loaded, 16)
            for g, window in enumerate(WINDOWS):
                nc.gpsimd.memset(inv_count[:, g, PAD:SEQ], 1.0 / window)
            nc.gpsimd.iota(inv_count[:, 3, 0:PAD], pattern=[[1, PAD]], base=1, channel_multiplier=0,
                           allow_small_or_imprecise_dtypes=True).then_inc(counts_ready, 1)
            nc.gpsimd.memset(ones[:, :], 1.0)
            chained(nc.gpsimd.memset(mask[:, :], 0.0))
            nc.gpsimd.memset(mask[0:CHUNK, CHUNK:P], MASKED)
            nc.gpsimd.memset(mask[0:CHUNK, P + 3 * CHUNK:P + 4 * CHUNK], MASKED)
            nc.gpsimd.memset(mask[CHUNK:P, P:P + CHUNK], MASKED).then_inc(consts_ready, 1)
            pool.wait_ge(h_ready, 4)
            pool.wait_ge(consts_ready, 1)
            pool.dma_start(pool_w[:, :, :, :], a["pool_w"][0].rearrange("g (k p) n -> p g k n", p=P)
                           ).then_inc(pool_w_loaded, 16)
            nc.gpsimd.memset(conv_in[:, :, 0:TAPS - 1], 0.0)
            nc.gpsimd.memset(pool_in[:, :, 0:PAD], 0.0).then_inc(pads_ready, 1)
            for i in range(2):
                pool.wait_ge(*(freed(0) if i == 0 else (a1_copied, 1)))
                pool.wait_ge(*freed(1 + i))
                nc.gpsimd.tensor_tensor(glu_a[i][:, :, :], glu_a[i][:, :, :], glu_b[:, :, :], ALU.mult
                                        ).then_inc(glu_ready, 1)
            pool.wait_ge(inv_ready, 1)
            for i in range(2):
                pool.wait_ge(u_copied, i + 1)
                for g in (2 * i, 2 * i + 1):
                    u = pool_in[:, 2 * g:2 * g + 2, :]
                    src, reach = u, 1
                    for step in range(g + 1):
                        dst = (win_a, win_b)[step % 2]
                        lo = 2 * reach - 1
                        chained(nc.gpsimd.tensor_tensor(dst[:, :, lo:PAD + SEQ], src[:, :, lo:PAD + SEQ],
                                                        src[:, :, lo - reach:PAD + SEQ - reach], ALU.add))
                        src, reach = dst, 2 * reach
                    sums = src[:, :, PAD:PAD + SEQ]
                    chained(nc.gpsimd.tensor_tensor(sums, sums,
                                                    inv_count[:, g:g + 1, :].broadcast_to([P, 2, SEQ]), ALU.mult))
                    tokens = u[:, :, PAD:PAD + SEQ]
                    last = nc.gpsimd.tensor_tensor(tokens, sums, tokens, ALU.subtract)
                    if g == 2 * i:
                        chained(last)
                last.then_inc(mixed_ready, 1)
                pool.wait_ge(mixed_ready, i + 1)
            pool.wait_ge(glu_copied, 2)
            pool.wait_ge(u_t, 2)
            tiles = slice(DVE_TILES, BT)
            width = BT - DVE_TILES

            def wide(column):
                return column.unsqueeze(2).broadcast_to([P, width, SEQ])

            for k in range(TAPS):
                product = tap_prod[:, :, :] if k else conv_acc[:, tiles, :]
                chained(nc.gpsimd.tensor_tensor(product, conv_in[:, tiles, k:k + SEQ],
                                                wide(taps[:, k * BT + DVE_TILES:(k + 1) * BT]), ALU.mult))
                if k:
                    chained(nc.gpsimd.tensor_tensor(conv_acc[:, tiles, :], conv_acc[:, tiles, :], product, ALU.add))
            nc.gpsimd.tensor_tensor(conv_acc[:, tiles, :], conv_acc[:, tiles, :],
                                    wide(vec[:, V_DW_B + DVE_TILES:V_DW_B + BT]), ALU.add).then_inc(conv_pool, 1)
            pool.wait_ge(y_t, 4)
            pool.dma_start(gate_rows[:, :], a["b_ada"][0, 2 * D_MODEL:3 * D_MODEL].partition_broadcast(P)
                           ).then_inc(gate_b_loaded, 16)
            pool.wait_ge(used, M_CONVB)
            pool.dma_start(x_res[:, :, :], x_rows).then_inc(x_res_loaded, 16)
            pool.wait_ge(merged_ready, 8)
            pool.dma_start(final_rows[:, :], a["final_g"].partition_broadcast(P)).then_inc(final_loaded, 16)

        @block.scalar
        def _(act):
            def split(slot, raw_slot, full, free=None):
                act.wait_ge(loaded[raw_slot], full)
                if free is not None:
                    act.wait_ge(used, free)
                nc.scalar.activation(wh[:, slot], raw[:, raw_slot], ACT.Copy).then_inc(high_done, 1)

            def split_at(m):
                if m < M_END:
                    g = split_g(m)
                    split(m % RING, g % RING, 16 * (g // RING + 1), m - RING + 1 if m >= RING else None)

            def evacuate(n, dst, func):
                act.wait_ge(used, CHUNK_END[n])
                nc.scalar.activation(dst, acc[n % 2][:, :, :], func).then_inc(acc_free[n % 2], 1)

            def spread(dst, src, ready, count, signal):
                act.wait_ge(ready, count)
                nc.scalar.activation(dst, src, ACT.Copy).then_inc(signal, 1)

            act.wait_ge(c_loaded, 16)
            nc.scalar.activation(c_act, c_in, ACT.Silu).then_inc(c_ready, 1)
            act.wait_ge(x_loaded, 16)
            for h in range(TH):
                if h:
                    act.wait_ge(x_squared, h)
                nc.scalar.activation(square_out[:, :], x_tok[:, h, :], ACT.Square,
                                     accum_out=x_sum[:, h:h + 1]).then_inc(x_squared, 1)
            act.wait_ge(var_ready, 1)
            nc.scalar.activation(x_rstd, x_var, ACT.Sqrt).then_inc(root_ready, 1)
            for b in range(4):
                spread(x_chan[:, 4 * b:4 * b + 4, :], x_side(b), x_t, b + 1, x_copied)
            for q in range(4):
                if q:
                    split_at(3 * q - 3)
                spread(shift_row[:, :], pb[0:1, 0:COLS], shift_done, RING * (q + 1), shift_copied)
                if q:
                    split_at(3 * q - 2)
                act.wait_ge(mod_ready, q + 1)
                for t in range(PK):
                    k = PK * q + t
                    last = nc.scalar.activation(act_h[:, k, :], x_chan[:, k, :], ACT.Identity,
                                                scale=mod_scale[:, t:t + 1], bias=mod_shift[:, t:t + 1])
                last.then_inc(h_high, 1)
                if q:
                    split_at(3 * q - 1)
            for m in range(9, OPENING):
                split_at(m)

            def softmax_exp(u):
                width = P * (u % 2 + 1)
                act.wait_ge(max_ready, u + 1)
                for g in range(GROUP):
                    cols = slice(g * width, (g + 1) * width)
                    nc.scalar.activation(probs[:, cols], probs[:, cols], ACT.Exp, bias=neg_max[:, g:g + 1],
                                         accum_out=denom[:, g:g + 1])
                nc.scalar.activation(sink_exp, sink_exp, ACT.Exp).then_inc(exp_done, 1)

            for m in range(OPENING - RING, M_ATTN):
                if m == 9:
                    evacuate(0, glu_a[0][:, :, :], ACT.Copy)
                if m == 10:
                    evacuate(1, glu_b[:, :, :], ACT.Sigmoid)
                if m == 11:
                    act.wait_ge(used, OPENING)
                    nc.scalar.activation(glu_a[1][:, :, :], pa[:, :].rearrange("p (h c) -> p h c", h=TH), ACT.Copy
                                         ).then_inc(a1_copied, 1)
                if m == 15:
                    act.wait_ge(glu_ready, 1)
                    evacuate(2, glu_b[:, :, :], ACT.Sigmoid)
                if m in (12, 17):
                    i = m // 17
                    if i == 0:
                        act.wait_ge(pads_ready, 1)
                    spread(conv_in[:, 4 * i:4 * i + 4, TAPS - 1:TAPS - 1 + SEQ],
                           (pb, pa)[i][:, :].rearrange("p (t s) -> p t s", t=4), glu_t, i + 1, glu_copied)
                if m in (19, 23):
                    if m == 23:
                        act.wait_ge(u_t, 1)
                    else:
                        act.wait_ge(glu_t, 2)
                    evacuate(chunk_of(m), u_tok[:, :, :], ACT.Copy)
                if m in (21, 25):
                    i = (m - 21) // 4
                    spread(pool_in[:, 4 * i:4 * i + 4, PAD:PAD + SEQ],
                           (pb, pa)[i][:, :].rearrange("p (t s) -> p t s", t=4), u_t, i + 1, u_copied)
                if m == 27:
                    evacuate(chunk_of(m), kv_tok[:, :, :], ACT.Copy)
                if m == 29:
                    spread(k_chan[:, :, :], pb[:, 0:COLS].rearrange("p (t s) -> p t s", t=2), k_t, 1, k_copied)
                if m in (31, 35):
                    if m == 35:
                        act.wait_ge(q_t, 1)
                    else:
                        act.wait_ge(glu_t, 2)
                    n = chunk_of(m)
                    act.wait_ge(used, CHUNK_END[n])
                    for h in range(TH):
                        last = nc.scalar.activation(
                            q_tok[:, h, :].rearrange("p (g k d) -> p k g d", k=2, g=GROUP),
                            acc[n % 2][:, h, :].rearrange("p (k g d) -> p k g d", k=2, g=GROUP), ACT.Copy)
                    last.then_inc(acc_free[n % 2], 1)
                if m in (33, 37):
                    i = (m - 33) // 4
                    if i == 0:
                        act.wait_ge(pool_mm, 2)
                    spread(q_chan[:, i, :, :], (pb, pa)[i][:, :].rearrange("p (t s) -> p t s", t=4),
                           q_t, i + 1, q_copied)
                if m in (39, 43):
                    act.wait_ge(q_t, 2)
                    evacuate(chunk_of(m), zs_attn[:, :, bass.ts((m - 39) // 4, COLS)], ACT.Silu)
                if m in (47, 51):
                    if m == 51:
                        act.wait_ge(pool_z_used, 1)
                    evacuate(chunk_of(m), pool_silu[:, :, :], ACT.Silu)
                if m in (55, 59):
                    act.wait_ge(conv_pool, 1)
                    evacuate(chunk_of(m), zs_conv[:, :, bass.ts((m - 55) // 4, COLS)], ACT.Silu)
                if 40 <= m <= 54 and m % 2 == 0:
                    u = (m - 40) // 2
                    width = COLS * (u % 2 + 1)
                    act.wait_ge(probs_td, u + 1)
                    nc.scalar.activation(probs_t[:, :, :].rearrange("p k c -> p (k c)")[:, 0:width],
                                         pb[:, 0:width], ACT.Copy).then_inc(probs_copied, 1)
                if 38 <= m <= 52 and m % 2 == 0:
                    softmax_exp((m - 38) // 2)
                if m == 54:
                    act.wait_ge(ln_centered, 1)
                    act.wait_ge(pool_z_used, 2)
                    nc.scalar.activation(squares[:, :, :], conv_acc[:, :, :], ACT.Square).then_inc(ln_squared, 1)
                if m == 57:
                    act.wait_ge(var_ready, 2)
                    nc.scalar.activation(ln_rstd, ln_stat[:, :], ACT.Sqrt).then_inc(root_ready, 1)
                    act.wait_ge(ln_scaled, 1)
                    for t in range(BT):
                        last = nc.scalar.activation(squares[:, t, :], conv_acc[:, t, :], ACT.Silu,
                                                    scale=vec[:, V_LN_G + t:V_LN_G + t + 1],
                                                    bias=vec[:, V_LN_B + t:V_LN_B + t + 1])
                    last.then_inc(ln_silu, 1)
                if m == 59:
                    act.wait_ge(ln_silu, 1)
                    act.wait_ge(attn_ready, 8)
                    nc.scalar.activation(s0_h[:, :, :], squares[:, :, :], ACT.Copy).then_inc(ln_high, 1)
                if m in (56, 57):
                    b = m - 56
                    spread(s1_h[:, 4 * b:4 * b + 4, :], (pb, pa)[b][:, :].rearrange("p (t s) -> p t s", t=4),
                           y_t, b + 1, y_high)
                if m < M_ATTN - 1:
                    split_at(m + RING)

            def branch_loop(b, m0, g0, step, n0):
                with act.Fori(0, 2) as it:
                    for k in range(12):
                        ahead = place(k + 3, step)
                        split((k + 3) % RING, ahead % RING, it * (4 * step) + 16 * ((g0 + ahead) // RING + 1),
                              it * 12 + (m0 + k))
                        if k in (3, 9):
                            n = n0 + 2 * (k // 6)
                            act.wait_ge(used, it * 12 + (m0 + k + 1))
                            act.wait_ge(acc_free[(n - 1) % 2], it * 2 + ((n - 1) // 2 + 1))
                            nc.scalar.activation(gate_sig[:, :, :], acc[n % 2][:, :, :], ACT.Sigmoid
                                                 ).then_inc(acc_free[n % 2], 1)

            act.wait_ge(y_t, 2)
            branch_loop(*ATTN_LOOP)
            for m in range(M_PW, M_POOLB):
                split_at(m + 3)
                if m in (84, 85):
                    b = m - 84
                    act.wait_ge(y_t, 3 + b)
                    for t in range(4):
                        k = 4 * b + t
                        last = nc.scalar.activation(s1_h[:, k, :], (pa, pb)[b][:, bass.ts(t, SEQ)], ACT.Copy,
                                                    scale=vec[:, V_POOL_SCALE + k:V_POOL_SCALE + k + 1])
                    last.then_inc(y_high, 1)
            branch_loop(*POOL_LOOP)
            for b in range(2):
                spread(s0_h[:, 4 * b:4 * b + 4, :], (pa, pb)[b][:, :].rearrange("p (t s) -> p t s", t=4),
                       y_t, 5 + b, y_high)
            branch_loop(*CONV_LOOP)
            for j in range(4):
                if j == 2:
                    split_at(M_OUT + 3)
                spread(act_h[:, 4 * j:4 * j + 4, :], (pa, pb)[j % 2][:, :].rearrange("p (t s) -> p t s", t=4),
                       y_t, 7 + j, y_high)

            def square_result(j, h, ready):
                act.wait_ge(res_ready, ready)
                if j or h:
                    act.wait_ge(res_squared, TH * j + h)
                nc.scalar.activation(square_dump, x_res[:, h, bass.ts(j, COLS)], ACT.Square,
                                     accum_out=out_sums[:, 4 * h + j:4 * h + j + 1]).then_inc(res_squared, 1)

            nc.scalar.activation(out_rstd, x_var, ACT.Sqrt)
            for m in range(M_OUT, M_END):
                if m in (140, 144, 148):
                    j = (m - 140) // 4
                    for h in range(TH):
                        square_result(j, h, j + 1)
                split_at(m + RING)
            for h in range(TH):
                square_result(3, h, 4 + h)
                act.wait_ge(var_ready, 3 + h)
                nc.scalar.activation(out_rstd[:, h:h + 1], out_sum[:, h:h + 1], ACT.Sqrt).then_inc(root_ready, 1)
                act.wait_ge(rstd_ready, h + 1)
                half = x_res[:, h, HALF:D_MODEL]
                nc.scalar.activation(half, half, ACT.Copy, scale=out_rstd[:, h:h + 1]).then_inc(out_high, 1)
                act.wait_ge(out_high, h + 1)
                act.dma_start(out_rows[:, h, HALF:D_MODEL], half).then_inc(stored, 16)

        @block.vector
        def _(dve):
            count = [0]

            def chained(ins):
                count[0] += 1
                ins.then_inc(dve_chain, 1)
                dve.wait_ge(dve_chain, count[0])

            def split(slot, raw_slot, highs):
                dve.wait_ge(high_done, highs)
                nc.vector.tensor_tensor(wl[:, slot], raw[:, raw_slot], wh[:, slot].bitcast(F32), ALU.subtract
                                        ).then_inc(raw_done, 1)

            def split_at(m):
                if m < M_END:
                    split(m % RING, split_g(m) % RING, m + 1)

            def low_halves(b, dst_h, dst_l, src):
                dve.wait_ge(y_high, b + 1)
                nc.vector.tensor_tensor(dst_l, src[:, :].rearrange("p (t s) -> p t s", t=4),
                                        dst_h.bitcast(F32), ALU.subtract).then_inc(y_ready, 1)

            def inverse_root(root, var, tmp, number):
                dve.wait_ge(root_ready, number)
                chained(nc.vector.reciprocal(root, root))
                chained(nc.vector.scalar_tensor_tensor(tmp, root, -0.5, root, ALU.mult, ALU.mult))
                chained(nc.vector.tensor_tensor(tmp, tmp, var, ALU.mult))
                chained(nc.vector.scalar_tensor_tensor(root, tmp, 1.5, root, ALU.add, ALU.mult))

            dve.wait_ge(c_ready, 1)
            dve.wait_ge(x_squared, 2)
            nc.vector.tensor_scalar(x_var, x_sum, 1.0 / D_MODEL, EPS, ALU.mult, ALU.add).then_inc(var_ready, 1)
            dve.wait_ge(var_ready, 1)
            inverse_root(x_rstd, x_var, newton, 1)
            for h in range(TH):
                last = nc.vector.tensor_scalar(x_tok[:, h, :], x_tok[:, h, :], x_rstd[:, h:h + 1], None, ALU.mult)
            last.then_inc(x_scaled, 1)

            def vectors():
                dve.wait_ge(vec_t, 1)
                nc.vector.tensor_copy(vec[:, :], pa[:, 0:V_ROWS])
                nc.vector.tensor_copy(taps[:, :].rearrange("p (i r) -> p i r", i=2),
                                      pa[:, 128:640].rearrange("p (i r) -> p i r", i=2)[:, :, 0:124]
                                      ).then_inc(vec_ready, 1)
                dve.wait_ge(vec_ready, 1)
                scale_b = vec[:, V_B_ADA + KT:V_B_ADA + 2 * KT]
                chained(nc.vector.tensor_scalar(scale_b, scale_b, 1.0, None, ALU.add))

            for q in range(4):
                if q:
                    dve.wait_ge(mod_t, q)
                for i in range(RING):
                    if q and i == RING - 1:
                        split_at(3 * q - 3)
                    g = OPEN.index(("scale", q, i))
                    dve.wait_ge(loaded[g % RING], 16 * (g // RING + 1))
                    for t in range(PK):
                        src, column = raw[:, g % RING, t, :], c_act[:, PK * i + t:PK * i + t + 1]
                        if i == 0 and t == 0:
                            last = nc.vector.tensor_scalar(ada_sums[:, :], src, column, None, ALU.mult)
                        else:
                            last = nc.vector.scalar_tensor_tensor(ada_sums[:, :], src, column, ada_sums[:, :],
                                                                  ALU.mult, ALU.add)
                        if t < PK - 1:
                            chained(last)
                    last.then_inc(raw_done, 1)
                    if q == 0 and i == 2:
                        vectors()
                    if i < RING - 1:
                        dve.wait_ge(raw_done, freeing(g)[1])
                if q:
                    dve.wait_ge(h_high, q)
                    dve.wait_ge(h_ready, q)
                dve.wait_ge(mod_t, q + 1)
                k = PK * q
                chained(nc.vector.tensor_reduce(mod_scale, pb[:, COLS:2 * COLS].rearrange("p (t c) -> p t c", t=PK),
                                                AX, ALU.add))
                chained(nc.vector.tensor_tensor(mod_scale, mod_scale, vec[:, V_B_ADA + KT + k:V_B_ADA + KT + k + 4],
                                                ALU.add))
                nc.vector.tensor_tensor(mod_shift, pb[:, 0:PK], vec[:, V_B_ADA + k:V_B_ADA + k + 4], ALU.add)
                nc.vector.tensor_tensor(mod_scale, mod_scale, vec[:, V_NORM_G + k:V_NORM_G + k + 4], ALU.mult
                                        ).then_inc(mod_ready, 1)
                dve.wait_ge(mod_ready, q + 1)
                if q == 0:
                    dve.wait_ge(x_copied, 4)
                for t in range(PK):
                    last = nc.vector.tensor_scalar(h_tmp[:, t, :], x_chan[:, k + t, :], mod_scale[:, t:t + 1],
                                                   mod_shift[:, t:t + 1], ALU.mult, ALU.add)
                chained(last)
                dve.wait_ge(h_high, q + 1)
                nc.vector.tensor_tensor(act_l[:, k:k + 4, :], h_tmp[:, :, :], act_h[:, k:k + 4, :].bitcast(F32),
                                        ALU.subtract).then_inc(h_ready, 1)
                if q == 0:
                    dve.wait_ge(counts_ready, 1)
                    for g in range(4):
                        chained(nc.vector.tensor_scalar(inv_count[:, g, 0:PAD], inv_count[:, 3, 0:PAD],
                                                        float(WINDOWS[g]), None, ALU.min))
                    nc.vector.reciprocal(inv_count[:, :, 0:PAD], inv_count[:, :, 0:PAD]).then_inc(inv_ready, 1)
                if q:
                    split_at(3 * q - 2)
                    split_at(3 * q - 1)
            for m in range(9, OPENING):
                split_at(m)

            def conv_tap(i):
                pair, rest = i // (2 * TAPS), i % (2 * TAPS)
                k, t = rest // 2, 2 * pair + rest % 2
                if i == 0:
                    dve.wait_ge(glu_copied, 1)
                if pair == 2 and rest == 0:
                    dve.wait_ge(glu_copied, 2)
                window, tap = conv_in[:, t, k:k + SEQ], taps[:, k * BT + t:k * BT + t + 1]
                if k == 0:
                    ins = nc.vector.tensor_scalar(conv_acc[:, t, :], window, tap,
                                                  vec[:, V_DW_B + t:V_DW_B + t + 1], ALU.mult, ALU.add)
                else:
                    dve.wait_ge(conv_dve, i - 1)
                    ins = nc.vector.scalar_tensor_tensor(conv_acc[:, t, :], window, tap, conv_acc[:, t, :],
                                                         ALU.mult, ALU.add)
                ins.then_inc(conv_dve, 1)

            def score_max(u):
                width = P * (u % 2 + 1)
                scores = pa[:, 0:GROUP * width].rearrange("p (g k) -> p g k", g=GROUP)
                masked = probs[:, 0:GROUP * width].rearrange("p (g k) -> p g k", g=GROUP)
                shown = mask[:, 0:P] if u % 2 == 0 else mask[:, P:P + SEQ]
                sink = sinks[:, GROUP * (u // 2):GROUP * (u // 2) + GROUP]
                dve.wait_ge(scores_done, u + 1)
                if u:
                    dve.wait_ge(probs_td, u)
                else:
                    dve.wait_ge(pool_mm, 2)
                    dve.wait_ge(sink_loaded, 16)
                    dve.wait_ge(consts_ready, 1)
                nc.vector.scalar_tensor_tensor(masked, scores, HEAD_DIM ** -0.5,
                                               shown.unsqueeze(1).broadcast_to([P, GROUP, width]),
                                               ALU.mult, ALU.add).then_inc(scores_read, 1)
                dve.wait_ge(scores_read, u + 1)
                chained(nc.vector.tensor_reduce(row_max, masked, AX, ALU.max))
                chained(nc.vector.tensor_tensor(row_max, row_max, sink, ALU.max))
                nc.vector.tensor_tensor(sink_exp, sink, row_max, ALU.subtract)
                nc.vector.tensor_scalar(neg_max, row_max, -1.0, None, ALU.mult).then_inc(max_ready, 1)

            def denominators(u):
                dve.wait_ge(exp_done, u + 1)
                chained(nc.vector.tensor_tensor(denom, denom, sink_exp, ALU.add))
                nc.vector.reciprocal(inv_den, denom).then_inc(denom_ready, 1)

            def attend(u):
                hkv, h = u // 2, u % 2
                dve.wait_ge(pv_done, u + 1)
                dve.wait_ge(denom_ready, u + 1)
                dve.wait_ge(*freed(8 + hkv // 2))
                for g in range(GROUP):
                    z = zs_attn[:, h, bass.ts(hkv * GROUP + g, HEAD_DIM)]
                    last = nc.vector.scalar_tensor_tensor(z, pb[:, bass.ts(g, HEAD_DIM)], inv_den[:, g:g + 1], z,
                                                          ALU.mult, ALU.mult)
                last.then_inc(attn_ready, 1)

            taps_done = 0
            for m in range(OPENING - RING, M_ATTN):
                if m in (27, 32):
                    i = m // 32
                    dve.wait_ge(pool_mm, i + 1)
                    nc.vector.tensor_copy(zs_pool[:, :, bass.ts(i, COLS)],
                                          pa[:, :].rearrange("p (h c) -> p h c", h=TH)).then_inc(pool_out, 1)
                if m in (47, 51):
                    i = (m - 47) // 4
                    half = zs_pool[:, :, bass.ts(i, COLS)]
                    dve.wait_ge(*freed(chunk_of(m)))
                    dve.wait_ge(pool_out, 2)
                    nc.vector.tensor_tensor(half, half, pool_silu[:, :, :], ALU.mult).then_inc(pool_z_used, 1)
                if 41 <= m <= 55 and m % 2:
                    attend((m - 41) // 2)
                if 38 <= m <= 52 and m % 2 == 0:
                    score_max((m - 38) // 2)
                if 39 <= m <= 53 and m % 2:
                    denominators((m - 39) // 2)
                if 13 <= m:
                    for i in range(taps_done, min(taps_done + TAP_STEP, DVE_TILES * TAPS)):
                        conv_tap(i)
                    taps_done = min(taps_done + TAP_STEP, DVE_TILES * TAPS)
                if m == 51:
                    assert taps_done == DVE_TILES * TAPS
                    dve.wait_ge(conv_dve, DVE_TILES * TAPS)
                    dve.wait_ge(conv_pool, 1)
                    nc.vector.tensor_reduce(ln_stat[:, :], conv_acc[:, :, :].rearrange("p t s -> p s t"), AX,
                                            ALU.add).then_inc(ln_partial, 1)
                if m == 54:
                    dve.wait_ge(ln_summed, 1)
                    chained(nc.vector.tensor_scalar(ln_stat[:, :], pa[:, 0:SEQ], 1.0 / BRANCH, None, ALU.mult))
                    nc.vector.tensor_tensor(conv_acc[:, :, :], conv_acc[:, :, :],
                                            ln_stat[:, :].unsqueeze(1).broadcast_to([P, BT, SEQ]), ALU.subtract
                                            ).then_inc(ln_centered, 1)
                if m == 55:
                    dve.wait_ge(ln_squared, 1)
                    nc.vector.tensor_reduce(ln_stat[:, :], squares[:, :, :].rearrange("p t s -> p s t"), AX,
                                            ALU.add).then_inc(ln_partial, 1)
                if m == 57:
                    dve.wait_ge(ln_sq_summed, 1)
                    nc.vector.tensor_scalar(ln_stat[:, :], pa[:, COLS:COLS + SEQ], 1.0 / BRANCH, EPS,
                                            ALU.mult, ALU.add).then_inc(var_ready, 1)
                    dve.wait_ge(var_ready, 2)
                    inverse_root(ln_rstd, ln_stat[:, :], ln_newton, 2)
                    nc.vector.tensor_tensor(conv_acc[:, :, :], conv_acc[:, :, :],
                                            ln_rstd.unsqueeze(1).broadcast_to([P, BT, SEQ]), ALU.mult
                                            ).then_inc(ln_scaled, 1)
                if m == 59:
                    dve.wait_ge(ln_high, 1)
                    nc.vector.tensor_tensor(s0_l[:, :, :], squares[:, :, :], s0_h[:, :, :].bitcast(F32),
                                            ALU.subtract).then_inc(ln_ready, 1)
                if m in (56, 57):
                    b = m - 56
                    tiles = slice(4 * b, 4 * b + 4)
                    low_halves(b, s1_h[:, tiles, :], s1_l[:, tiles, :], (pb, pa)[b])
                if m < M_ATTN - 1:
                    split_at(m + RING)

            def branch_loop(b, m0, g0, step, n0):
                gate0 = 2 if b == CONV_B else 0
                with dve.Fori(0, 2) as it:
                    for k in range(12):
                        split((k + 3) % RING, place(k + 3, step) % RING, it * 12 + (m0 + k + 4))
                        if step == 16 and k + 3 in GATE_AFTER:
                            i = GATE_AFTER.index(k + 3)
                            here = place(k + 3, step) + 1
                            dve.wait_ge(loaded[here % RING], it * (4 * step) + 16 * ((g0 + here) // RING + 1))
                            for t in range(PK):
                                column = c_act[:, PK * i + t:PK * i + t + 1]
                                src = raw[:, here % RING, t, :]
                                if i == 0 and t == 0:
                                    last = nc.vector.tensor_scalar(gate_sums[:, :], src, column, None, ALU.mult)
                                else:
                                    if t:
                                        dve.wait_ge(gate_summed, it * 12 + (12 * gate0 + 3 * i + t))
                                    else:
                                        before = place(GATE_AFTER[i - 1], step) + 1
                                        dve.wait_ge(raw_done, it * 16 + (g0 - SHIFTS + before + 1))
                                    last = nc.vector.scalar_tensor_tensor(gate_sums[:, :], src, column,
                                                                          gate_sums[:, :], ALU.mult, ALU.add)
                                last.then_inc(gate_summed if t < PK - 1 else raw_done, 1)
                        if step == 16 and k == 11:
                            dve.wait_ge(gate_rows_mm, it + (gate0 + 1))
                            dve.wait_ge(gate_b_loaded, 16)
                            row = gate_rows[:, bass.ds(it * COLS + COLS * gate0, COLS)]
                            nc.vector.tensor_tensor(row, row, pa[:, 0:COLS], ALU.add).then_inc(gate_added, 1)
                        if k in (5, 11):
                            n, j = n0 + 2 * (k // 6) + 1, k // 6
                            dve.wait_ge(acc_free[(n - 1) % 2], it * 2 + ((n - 1) // 2 + 1))
                            dve.wait_ge(used, it * 12 + (m0 + k + 1))
                            total = merged[:, :, bass.ds(it * (2 * COLS) + COLS * j, COLS)]
                            if b == ATTN_B:
                                nc.vector.tensor_tensor(total, acc[n % 2][:, :, :], gate_sig[:, :, :], ALU.mult
                                                        ).then_inc(acc_free[n % 2], 1)
                            else:
                                dve.wait_ge(raw_done, it * step + (g0 - SHIFTS + place(k + 2, step) + 1))
                                nc.vector.tensor_tensor(gated[:, :, :], acc[n % 2][:, :, :], gate_sig[:, :, :],
                                                        ALU.mult).then_inc(acc_free[n % 2], 1)
                                dve.wait_ge(acc_free[n % 2], it * 2 + (n // 2 + 1))
                                nc.vector.tensor_tensor(total, total, gated[:, :, :], ALU.add
                                                        ).then_inc(merged_ready, 1)

            branch_loop(*ATTN_LOOP)
            for m in range(M_PW, M_POOLB):
                split_at(m + 3)
                if m in (84, 85):
                    b = m - 84
                    dve.wait_ge(y_high, 3 + b)
                    for t in range(4):
                        k = 4 * b + t
                        last = nc.vector.scalar_tensor_tensor(s1_l[:, k, :], (pa, pb)[b][:, bass.ts(t, SEQ)],
                                                              vec[:, V_POOL_SCALE + k:V_POOL_SCALE + k + 1],
                                                              s1_h[:, k, :].bitcast(F32), ALU.mult, ALU.subtract)
                    last.then_inc(y_ready, 1)
                if m in (85, 87):
                    j = (m - 85) // 2
                    n = N_PW + j
                    half = zs_conv[:, :, bass.ts(j, COLS)]
                    dve.wait_ge(*freed(12 + j))
                    dve.wait_ge(used, CHUNK_END[n])
                    nc.vector.tensor_tensor(half, acc[n % 2][:, :, :], half, ALU.mult).then_inc(acc_free[n % 2], 1)
            branch_loop(*POOL_LOOP)
            for b in range(2):
                tiles = slice(4 * b, 4 * b + 4)
                low_halves(4 + b, s0_h[:, tiles, :], s0_l[:, tiles, :], (pa, pb)[b])
            branch_loop(*CONV_LOOP)
            for j in range(4):
                if j == 2:
                    split_at(M_OUT + 3)
                tiles = slice(4 * j, 4 * j + 4)
                low_halves(6 + j, act_h[:, tiles, :], act_l[:, tiles, :], (pa, pb)[j % 2])

            def residual(j):
                n = N_OUT + j
                cols = bass.ts(j, COLS)
                dve.wait_ge(used, CHUNK_END[n])
                if j:
                    dve.wait_ge(res_ready, j)
                nc.vector.tensor_tensor(out_tmp[:, :, :], acc[n % 2][:, :, :],
                                        gate_rows[:, cols].unsqueeze(1).broadcast_to([P, TH, COLS]), ALU.mult
                                        ).then_inc(acc_free[n % 2], 1)
                dve.wait_ge(*freed(n))
                nc.vector.tensor_tensor(x_res[:, :, cols], x_res[:, :, cols], out_tmp[:, :, :], ALU.add
                                        ).then_inc(res_ready, 1)

            def scale_result(j):
                cols = bass.ts(j, COLS)
                if j == 0:
                    dve.wait_ge(final_loaded, 16)
                dve.wait_ge(res_squared, TH * (j + 1))
                nc.vector.tensor_tensor(x_res[:, :, cols], x_res[:, :, cols],
                                        final_rows[:, cols].unsqueeze(1).broadcast_to([P, TH, COLS]), ALU.mult)

            dve.wait_ge(gate_added, 4)
            dve.wait_ge(x_res_loaded, 16)
            for m in range(M_OUT, M_END):
                if m in (139, 143, 147):
                    residual((m - M_OUT) // 4)
                if m in (142, 146, 150):
                    scale_result((m - 142) // 4)
                split_at(m + RING)
            cols = slice(3 * COLS, D_MODEL)
            for h in range(TH):
                rest = x_res[:, h, cols]
                dve.wait_ge(tile_summed, h + 1)
                chained(nc.vector.tensor_tensor(out_tmp[:, h, :], acc[(N_OUT + 3) % 2][:, h, :], gate_rows[:, cols],
                                                ALU.mult))
                nc.vector.tensor_tensor(rest, rest, out_tmp[:, h, :], ALU.add).then_inc(res_ready, 1)
                dve.wait_ge(res_squared, 3 * TH + h + 1)
                total = out_sum[:, h:h + 1]
                chained(nc.vector.tensor_reduce(total, out_sums[:, 4 * h:4 * h + 4], AX, ALU.add))
                nc.vector.tensor_scalar(total, total, 1.0 / D_MODEL, EPS, ALU.mult, ALU.add).then_inc(var_ready, 1)
                chained(nc.vector.tensor_tensor(rest, rest, final_rows[:, cols], ALU.mult))
                dve.wait_ge(var_ready, 3 + h)
                inverse_root(out_rstd[:, h:h + 1], total, newton[:, h:h + 1], 3 + h)
                nc.vector.engine_nop().then_inc(rstd_ready, 1)
                half = x_res[:, h, 0:HALF]
                nc.vector.tensor_scalar(half, half, out_rstd[:, h:h + 1], None, ALU.mult).then_inc(out_ready, 1)

        @block.tensor
        def _(pe):
            def piece(lhs_h, lhs_l, k0, slot, sums, count, first, last):
                pe.wait_ge(raw_done, count)
                for i in range(PK):
                    for h in range(TH):
                        tokens = slice(P * h, P * (h + 1))
                        begin, end = first and i == 0, last and i == PK - 1
                        xh, xl = lhs_h[:, k0 + i, tokens], lhs_l[:, k0 + i, tokens]
                        nc.tensor.matmul(sums[:, h, :], xh, wh[:, slot, i, :], start=begin, stop=False)
                        nc.tensor.matmul(sums[:, h, :], xh, wl[:, slot, i, :], start=False, stop=False)
                        ins = nc.tensor.matmul(sums[:, h, :], xl, wh[:, slot, i, :], start=False, stop=end)
                ins.then_inc(used, 1)

            def half_piece(lhs_h, lhs_l, k0, slot, sums, h, first, last):
                for i in range(PK):
                    tokens = slice(P * h, P * (h + 1))
                    begin, end = first and i == 0, last and i == PK - 1
                    xh, xl = lhs_h[:, k0 + i, tokens], lhs_l[:, k0 + i, tokens]
                    nc.tensor.matmul(sums[:, h, :], xh, wh[:, slot, i, :], start=begin, stop=False)
                    nc.tensor.matmul(sums[:, h, :], xh, wl[:, slot, i, :], start=False, stop=False)
                    ins = nc.tensor.matmul(sums[:, h, :], xl, wh[:, slot, i, :], start=False, stop=end)
                return ins

            def transpose4(dst, src, ready):
                for t in range(4):
                    for h in range(TH):
                        ins = nc.tensor.transpose(dst[:, SEQ * t + P * h:SEQ * t + P * (h + 1)],
                                                  src(h, t), ident[:, :])
                ins.then_inc(ready, 1)

            def block_of(buf, col=0):
                return lambda h, t: buf[:, h, col + P * t:col + P * (t + 1)]

            hidden = (act_h, act_l)
            slot0, slot1 = (s0_h, s0_l), (s1_h, s1_l)

            def shift_piece(q, i):
                g = OPEN.index(("shift", q, i))
                pe.wait_ge(loaded[g % RING], 16 * (g // RING + 1))
                if q and i == 0:
                    pe.wait_ge(mod_ready, q)
                for t in range(PK):
                    k = PK * i + t
                    ins = nc.tensor.matmul(pb[0:1, 0:COLS], c_act[:, k:k + 1], raw[:, g % RING, t, :],
                                           start=(k == 0), stop=(k == KT - 1))
                ins.then_inc(shift_done, 1)

            def modulation(q):
                pe.wait_ge(shift_copied, q + 1)
                for t in range(PK):
                    nc.tensor.transpose(pb[:, t:t + 1], shift_row[0:1, P * t:P * (t + 1)], ident[0:1, 0:1])
                pe.wait_ge(raw_done, freeing(OPEN.index(("scale", q, RING - 1)))[1])
                for t in range(PK):
                    ins = nc.tensor.transpose(pb[:, COLS + P * t:COLS + P * (t + 1)],
                                              ada_sums[:, P * t:P * (t + 1)], ident[:, :])
                ins.then_inc(mod_t, 1)

            def opening(q, c):
                m = 3 * q + c
                if c == 0:
                    pe.wait_ge(h_ready, q + 1)
                sums = acc[c] if c < 2 else pa[:, :].rearrange("p (h c) -> p h c", h=TH)
                piece(act_h, act_l, PK * q, m % RING, sums, freeing(split_g(m))[1], q == 0, q == 3)

            pe.wait_ge(c_ready, 1)
            shift_piece(0, 0)
            pe.wait_ge(ident_ready, 1)
            pe.wait_ge(x_scaled, 1)
            for b in range(4):
                if b >= 2:
                    pe.wait_ge(x_copied, b - 1)
                dst = x_side(b)
                for t in range(4):
                    for h in range(TH):
                        ins = nc.tensor.transpose(dst[:, t, P * h:P * (h + 1)],
                                                  x_tok[:, h, COLS * b + P * t:COLS * b + P * (t + 1)], ident[:, :])
                ins.then_inc(x_t, 1)
            shift_piece(0, 1)
            pe.wait_ge(vec_loaded, 16 * 6)
            pe.wait_ge(tap_loaded, 16 * 2)
            nc.tensor.transpose(pa[:, 0:V_ROWS], vec_rows[0:V_ROWS, :], ident[0:V_ROWS, 0:V_ROWS])
            nc.tensor.transpose(pa[:, 128:252], tap_rows[0:124, 0, :], ident[0:124, 0:124])
            nc.tensor.transpose(pa[:, 384:508], tap_rows[0:124, 1, :], ident[0:124, 0:124]).then_inc(vec_t, 1)
            shift_piece(0, 2)
            shift_piece(0, 3)
            modulation(0)
            for i in range(RING):
                shift_piece(1, i)
            modulation(1)
            pe.wait_ge(x_copied, 4)
            pe.wait_ge(vec_ready, 1)
            for q in (2, 3):
                opening(q - 2, 0)
                shift_piece(q, 0)
                opening(q - 2, 1)
                shift_piece(q, 1)
                shift_piece(q, 2)
                opening(q - 2, 2)
                shift_piece(q, 3)
                modulation(q)
            for q in (2, 3):
                for c in range(3):
                    opening(q, c)

            def stream(m, lhs, k0, n, first, last):
                if first:
                    pe.wait_ge(acc_free[n % 2], n // 2)
                piece(*lhs, k0, m % RING, acc[n % 2], freeing(split_g(m))[1], first, last)

            def unit_scores(u):
                hkv, h = u // 2, u % 2
                rows = slice(HEAD_DIM * (hkv % 2), HEAD_DIM * (hkv % 2 + 1))
                width = P * (h + 1)
                if u:
                    pe.wait_ge(scores_read, u)
                pe.wait_ge(q_copied, 2)
                pe.wait_ge(k_copied, 1)
                for g in range(GROUP):
                    ins = nc.tensor.matmul(pa[:, g * width:(g + 1) * width],
                                           q_chan[rows, hkv // 2, g, P * h:P * (h + 1)],
                                           k_chan[rows, hkv // 2, 0:width], start=True, stop=True)
                ins.then_inc(scores_done, 1)

            def unit_transpose(u):
                h = u % 2
                width = P * (h + 1)
                pe.wait_ge(exp_done, u + 1)
                if u:
                    pe.wait_ge(attn_ready, u)
                for kt in range(h + 1):
                    for g in range(GROUP):
                        ins = nc.tensor.transpose(pb[:, COLS * kt + P * g:COLS * kt + P * (g + 1)],
                                                  probs[:, g * width + P * kt:g * width + P * (kt + 1)], ident[:, :])
                ins.then_inc(probs_td, 1)

            def unit_values(u):
                hkv, h = u // 2, u % 2
                pe.wait_ge(probs_copied, u + 1)
                for g in range(GROUP):
                    for kt in range(h + 1):
                        ins = nc.tensor.matmul(pb[:, HEAD_DIM * g:HEAD_DIM * (g + 1)],
                                               probs_t[:, kt, P * g:P * (g + 1)],
                                               kv_tok[:, kt, SEQ + HEAD_DIM * hkv:SEQ + HEAD_DIM * (hkv + 1)],
                                               start=(kt == 0), stop=(kt == h))
                ins.then_inc(pv_done, 1)

            def column_sums(dst, ready):
                nc.tensor.matmul(dst, ones[:, :], ln_stat[:, :], start=True, stop=True).then_inc(ready, 1)

            for m in range(OPENING, M_ATTN):
                n = chunk_of(m)
                stream(m, hidden, PK * (m % 4), n, m % 4 == 0, m % 4 == 3)
                if m in (12, 17):
                    i = m // 17
                    pe.wait_ge(glu_ready, i + 1)
                    if i:
                        pe.wait_ge(a1_copied, 1)
                    else:
                        pe.wait_ge(mod_ready, 4)
                    transpose4((pb, pa)[i], block_of(glu_a[i]), glu_t)
                if m in (21, 25):
                    i = (m - 21) // 4
                    pe.wait_ge(*freed(3 + i))
                    pe.wait_ge(glu_copied, i + 1)
                    transpose4((pb, pa)[i], block_of(u_tok), u_t)
                if m in (27, 32):
                    i = m // 32
                    pe.wait_ge(mixed_ready, i + 1)
                    pe.wait_ge(pool_w_loaded, 16)
                    pe.wait_ge(u_copied, 2)
                    if i:
                        pe.wait_ge(pool_out, 1)
                    for h in range(TH):
                        for gg in range(2):
                            g = 2 * i + gg
                            for k in range(2):
                                lo = PAD + P * h
                                ins = nc.tensor.matmul(pa[:, COLS * h + SEQ * gg:COLS * h + SEQ * (gg + 1)],
                                                       pool_in[:, 2 * g + k, lo:lo + P], pool_w[:, g, k, :],
                                                       start=(k == 0), stop=(k == 1))
                    ins.then_inc(pool_mm, 1)
                if m == 29:
                    pe.wait_ge(*freed(5))
                    pe.wait_ge(u_copied, 1)
                    for t in range(2):
                        for h in range(TH):
                            ins = nc.tensor.transpose(pb[:, SEQ * t + P * h:SEQ * t + P * (h + 1)],
                                                      kv_tok[:, h, P * t:P * (t + 1)], ident[:, :])
                    ins.then_inc(k_t, 1)
                if m in (33, 37):
                    i = (m - 33) // 4
                    pe.wait_ge(*freed(6 + i))
                    if i:
                        pe.wait_ge(pool_out, 2)
                    else:
                        pe.wait_ge(k_copied, 1)
                    transpose4((pb, pa)[i], block_of(q_tok), q_t)
                if 40 <= m <= 54 and m % 2 == 0:
                    unit_transpose((m - 40) // 2)
                if 38 <= m <= 52 and m % 2 == 0:
                    unit_scores((m - 38) // 2)
                if 41 <= m <= 55 and m % 2:
                    unit_values((m - 41) // 2)
                if m == 53:
                    pe.wait_ge(ln_partial, 1)
                    pe.wait_ge(scores_read, 8)
                    column_sums(pa[:, 0:SEQ], ln_summed)
                if m == 56:
                    pe.wait_ge(ln_partial, 2)
                    column_sums(pa[:, COLS:COLS + SEQ], ln_sq_summed)
                if m in (56, 57):
                    b = m - 56
                    pe.wait_ge(attn_ready, 8)
                    if b:
                        pe.wait_ge(var_ready, 2)
                    transpose4((pb, pa)[b], block_of(zs_attn, COLS * b), y_t)

            def branch_loop(b, m0, g0, step, n0, lhs, ready):
                with pe.Fori(0, 2) as it:
                    for k in range(12):
                        if k == 4:
                            pe.wait_ge(y_ready, ready)
                        n = n0 + 2 * (k // 6) + (k % 6 >= 4)
                        first, last = k % 6 in (0, 4), k % 6 in (3, 5)
                        if first:
                            pe.wait_ge(acc_free[n % 2], it * 2 + n // 2)
                        left, k0 = (hidden, PK * (k % 6)) if k % 6 < 4 else (lhs, PK * (k % 6 - 4))
                        piece(*left, k0, k % RING, acc[n % 2], it * step + (g0 - SHIFTS + place(k, step) + 1),
                              first, last)
                        if step == 16 and k == 10:
                            pe.wait_ge(raw_done, it * 16 + (g0 - SHIFTS + 16))
                            nc.tensor.matmul(pa[:, 0:COLS], ones[:, :], gate_sums[:, :], start=True, stop=True
                                             ).then_inc(gate_rows_mm, 1)

            branch_loop(*ATTN_LOOP, slot1, 2)
            pe.wait_ge(ln_ready, 1)
            for m in range(M_PW, M_POOLB):
                j, i = (m - M_PW) // 2, (m - M_PW) % 2
                stream(m, slot0, PK * i, N_PW + j, i == 0, i == 1)
                if m in (84, 85):
                    b = m - 84
                    pe.wait_ge(pool_z_used, 2)
                    if b == 0:
                        pe.wait_ge(y_ready, 2)
                    transpose4((pa, pb)[b], block_of(zs_pool, COLS * b), y_t)
            branch_loop(*POOL_LOOP, slot1, 4)
            for b in range(2):
                pe.wait_ge(*freed(N_PW + b))
                if b == 0:
                    pe.wait_ge(gate_added, 2)
                else:
                    pe.wait_ge(y_ready, 4)
                transpose4((pa, pb)[b], block_of(zs_conv, COLS * b), y_t)
            branch_loop(*CONV_LOOP, slot0, 6)

            def merged_by_channels(j):
                pe.wait_ge(merged_ready, 8 if j == 3 else 7 if j == 2 else 6)
                if j == 0:
                    pe.wait_ge(gate_added, 4)
                else:
                    pe.wait_ge(y_ready, 5 + j)
                transpose4((pa, pb)[j % 2], block_of(merged, COLS * j), y_t)

            merged_by_channels(0)
            merged_by_channels(1)
            for m in range(M_OUT, M_END - RING):
                j, i = (m - M_OUT) // 4, (m - M_OUT) % 4
                if j == 0:
                    pe.wait_ge(y_ready, 7 + i)
                stream(m, hidden, PK * i, N_OUT + j, i == 0, i == 3)
                if m in (M_OUT, M_OUT + 1):
                    merged_by_channels(2 + m - M_OUT)
            pe.wait_ge(*freed(N_OUT + 1))
            for h in range(TH):
                for i in range(RING):
                    m = M_END - RING + i
                    if h == 0:
                        pe.wait_ge(raw_done, freeing(split_g(m))[1])
                    ins = half_piece(*hidden, PK * i, m % RING, acc[(N_OUT + 3) % 2], h, i == 0, i == RING - 1)
                ins.then_inc(tile_summed, 1)


_INPUTS = ["x", "c", "norm_g", "w_ada", "b_ada", "w_in", "pool_w", "pool_scale", "attn_sink", "conv_dw",
           "conv_dw_b", "conv_ln_g", "conv_ln_b", "conv_pw", "w_branch_pool", "w_branch_attn",
           "w_branch_conv", "w_out", "final_g"]


def kernel(**inputs):
    import numpy as np
    import concourse.bacc as bacc
    from concourse.bass_utils import run_bass_kernel_spmd as run

    nc = bacc.Bacc("TRN2", target_bir_lowering=False, num_devices=1)
    arrays, args = {}, {}
    for name in _INPUTS:
        array = np.ascontiguousarray(inputs[name])
        arrays[f"in_{name}"] = array
        args[name] = nc.dram_tensor(f"in_{name}", array.shape, mybir.dt.from_np(array.dtype),
                                    kind="ExternalInput").ap()
    out = nc.dram_tensor("out", (1, SEQ, D_MODEL), mybir.dt.float32, kind="ExternalOutput").ap()
    program(nc, args, out)
    result = run(nc, [arrays], core_ids=[0])
    return result.results[0]["out"]
```
